# Optimizing a Trainium2 kernel written in Bass

```python
import jax, jax.numpy as jnp
from jax import lax
import numpy as np

D_MODEL = 1024
BATCH = 1
SEQ = 512
DEPTH = 1

N_SUBLAYERS = 3
N_MOD = 3
D_FF = 2816
FFN_RES = 0.5
MLA_HEADS = 8
MLA_Q_LORA = 256
MLA_KV_LORA = 128
MLA_NOPE = 64
MLA_ROPE = 32
MLA_V = 64
MLA_THETA = 10000.0
Q_BLOCK = 128
DIL_PATTERNS = ((128, 1), (512, 4), (2048, 16))
N_DIL_GROUPS = 3
DIL_HEADS_PER_GROUP = 4
DIL_HEAD_DIM = 64
ROPE_THETA = 500000.0
ROPE_PART = DIL_HEAD_DIM // 4
DIL_QKV = 3 * N_DIL_GROUPS * DIL_HEADS_PER_GROUP * DIL_HEAD_DIM
IN_SPLITS = (MLA_Q_LORA, MLA_KV_LORA, MLA_ROPE, DIL_QKV, D_MODEL, D_MODEL)
D_IN = MLA_Q_LORA + MLA_KV_LORA + MLA_ROPE + DIL_QKV + 2 * D_MODEL
NORM_EPS = 1e-6
NEG_INF = -1e30

kernel_name = 'hybrid_mla_dilated_macaron_block'

def rms_norm(x, g):
    xf = x.astype(jnp.float32)
    y = xf * lax.rsqrt(jnp.mean(xf * xf, axis=-1, keepdims=True) + NORM_EPS)
    return (y * g.astype(jnp.float32)).astype(x.dtype)

def modulate(x, shift, scale):
    return x * (1 + scale[:, None, :]) + shift[:, None, :]

def rope_cos_sin(positions, dim, theta):
    inv = theta ** (-jnp.arange(0, dim, 2, dtype=jnp.float32) / dim)
    ang = positions.astype(jnp.float32)[..., None] * inv
    return jnp.cos(ang), jnp.sin(ang)

def apply_rope(t, cos, sin):
    half = t.shape[-1] // 2
    t1 = t[..., :half].astype(jnp.float32)
    t2 = t[..., half:].astype(jnp.float32)
    return jnp.concatenate([t1 * cos - t2 * sin, t2 * cos + t1 * sin], axis=-1).astype(t.dtype)

def partial_rope(t, cos, sin):
    return jnp.concatenate([apply_rope(t[..., :ROPE_PART], cos, sin), t[..., ROPE_PART:]], axis=-1)

def swiglu(h, w_gate, w_up, w_down):
    return (jax.nn.silu(h @ w_gate) * (h @ w_up)) @ w_down

def mla_attention(q_nope, q_rope, k_nope, k_rope, v):
    B, S, H, _ = q_nope.shape
    nblk = S // Q_BLOCK
    scale = (MLA_NOPE + MLA_ROPE) ** -0.5

    def to_blocks(t):
        return jnp.moveaxis(t.reshape((B, nblk, Q_BLOCK) + t.shape[2:]), 1, 0)

    def block(qs):
        qn, qr = qs
        s = jnp.einsum('bqhe,bkhe->bhqk', qn, k_nope) + jnp.einsum('bqhr,bkr->bhqk', qr, k_rope)
        p = jax.nn.softmax(s.astype(jnp.float32) * scale, axis=-1).astype(v.dtype)
        return jnp.einsum('bhqk,bkhe->bqhe', p, v)

    o = lax.map(block, (to_blocks(q_nope), to_blocks(q_rope)))
    return jnp.moveaxis(o, 0, 1).reshape(B, S, H * MLA_V)

def dilated_window_attention(q, k, v, dilation, n_side):
    B, S, H, E = q.shape
    L = S // dilation
    W = n_side
    nb = -(-L // W)
    Lp = nb * W

    def stride_split(t):
        t = t.reshape(B, L, dilation, H, E).transpose(0, 2, 1, 3, 4)
        return jnp.pad(t, ((0, 0), (0, 0), (0, Lp - L), (0, 0), (0, 0)))

    def band(t):
        tp = jnp.pad(t, ((0, 0), (0, 0), (W, W), (0, 0), (0, 0))).reshape(B, dilation, nb + 2, W, H, E)
        return jnp.concatenate([tp[:, :, :-2], tp[:, :, 1:-1], tp[:, :, 2:]], axis=3)

    qb = stride_split(q).reshape(B, dilation, nb, W, H, E)
    kb = band(stride_split(k))
    vb = band(stride_split(v))
    s = jnp.einsum('bdnqhe,bdnkhe->bdnhqk', qb, kb).astype(jnp.float32) * (E ** -0.5)
    qi = jnp.arange(W)[:, None]
    kj = jnp.arange(3 * W)[None, :]
    rel = kj - W - qi
    t_k = (jnp.arange(nb)[:, None, None] - 1) * W + kj[None]
    valid = (jnp.abs(rel)[None] <= n_side) & (t_k >= 0) & (t_k < L)
    s = jnp.where(valid[:, None], s, NEG_INF)
    lse = jax.nn.logsumexp(s, axis=-1)
    p = jnp.exp(s - lse[..., None]).astype(v.dtype)
    o = jnp.einsum('bdnhqk,bdnkhe->bdnqhe', p, vb)
    o = o.reshape(B, dilation, Lp, H, E)[:, :, :L].transpose(0, 2, 1, 3, 4).reshape(B, S, H, E)
    lse = jnp.moveaxis(lse, 3, -1).reshape(B, dilation, Lp, H)[:, :, :L].transpose(0, 2, 1, 3).reshape(B, S, H)
    return o, lse

def token_mixer(u, cos_m, sin_m, cos_p, sin_p, w_in, g_cq, w_uq, g_ckv, w_ukv, w_o_mla, w_o_dil, w_out):
    B, S, _ = u.shape
    proj = u @ w_in
    offs = np.cumsum(IN_SPLITS)[:-1].tolist()
    c_q, c_kv, k_rope, qkv, gate_a, gate_b = jnp.split(proj, offs, axis=-1)

    q = (rms_norm(c_q, g_cq) @ w_uq).reshape(B, S, MLA_HEADS, MLA_NOPE + MLA_ROPE)
    q_nope = q[..., :MLA_NOPE]
    q_rope = apply_rope(q[..., MLA_NOPE:], cos_m[:, :, None], sin_m[:, :, None])
    kv = (rms_norm(c_kv, g_ckv) @ w_ukv).reshape(B, S, MLA_HEADS, MLA_NOPE + MLA_V)
    k_nope, v_mla = kv[..., :MLA_NOPE], kv[..., MLA_NOPE:]
    k_rope = apply_rope(k_rope, cos_m, sin_m)
    o_mla = mla_attention(q_nope, q_rope, k_nope, k_rope, v_mla)

    qkv = qkv.reshape(B, S, 3, N_DIL_GROUPS, DIL_HEADS_PER_GROUP, DIL_HEAD_DIM)
    cp, sp = cos_p[:, :, None], sin_p[:, :, None]
    outs, lses = [], []
    for g, (window, dil) in enumerate(DIL_PATTERNS):
        qg = partial_rope(qkv[:, :, 0, g], cp, sp)
        kg = partial_rope(qkv[:, :, 1, g], cp, sp)
        o, l = dilated_window_attention(qg, kg, qkv[:, :, 2, g], dil, window // (2 * dil))
        outs.append(o)
        lses.append(l)
    wts = jax.nn.softmax(jnp.stack(lses), axis=0).astype(u.dtype)
    o_dil = jnp.einsum('gbsh,gbshe->bshe', wts, jnp.stack(outs)).reshape(B, S, DIL_HEADS_PER_GROUP * DIL_HEAD_DIM)

    merged = jax.nn.sigmoid(gate_a) * (o_mla @ w_o_mla) + jax.nn.sigmoid(gate_b) * (o_dil @ w_o_dil)
    return merged @ w_out

def ffn_sublayer(x, shift, scale, gate, g_pre, w_gate, w_up, w_down, g_post):
    h = modulate(rms_norm(x, g_pre), shift, scale)
    y = rms_norm(swiglu(h, w_gate, w_up, w_down), g_post)
    return x + FFN_RES * gate[:, None, :] * y

def setup_inputs(seed: int = 0) -> dict:
    key = jax.random.key(seed)
    keys = jax.random.split(key, 25)
    f32 = jnp.float32

    def dense(k, shape, gain=1.0):
        return jax.random.normal(k, (DEPTH,) + shape, f32) * (gain * shape[0] ** -0.5)

    def gain_vec(k, dim):
        return 1.0 + 0.1 * jax.random.normal(k, (DEPTH, dim), f32)

    x = jax.random.normal(keys[0], (BATCH, SEQ, D_MODEL), f32)
    c = jax.random.normal(keys[1], (BATCH, D_MODEL), f32)
    positions = (jax.random.randint(keys[2], (BATCH, 1), 0, 2048, dtype=jnp.int32)
                 + jnp.arange(SEQ, dtype=jnp.int32)[None, :]).astype(jnp.int32)
    n_ada = N_SUBLAYERS * N_MOD * D_MODEL
    return {
        'x': x,
        'c': c,
        'positions': positions,
        'w_ada': dense(keys[3], (D_MODEL, n_ada), 0.5),
        'b_ada': 0.02 * jax.random.normal(keys[4], (DEPTH, n_ada), f32),
        'g_pre_ff1': gain_vec(keys[5], D_MODEL),
        'w_gate1': dense(keys[6], (D_MODEL, D_FF)),
        'w_up1': dense(keys[7], (D_MODEL, D_FF)),
        'w_down1': dense(keys[8], (D_FF, D_MODEL)),
        'g_post_ff1': gain_vec(keys[9], D_MODEL),
        'g_pre_mix': gain_vec(keys[10], D_MODEL),
        'w_in': dense(keys[11], (D_MODEL, D_IN)),
        'g_cq': gain_vec(keys[12], MLA_Q_LORA),
        'w_uq': dense(keys[13], (MLA_Q_LORA, MLA_HEADS * (MLA_NOPE + MLA_ROPE))),
        'g_ckv': gain_vec(keys[14], MLA_KV_LORA),
        'w_ukv': dense(keys[15], (MLA_KV_LORA, MLA_HEADS * (MLA_NOPE + MLA_V))),
        'w_o_mla': dense(keys[16], (MLA_HEADS * MLA_V, D_MODEL)),
        'w_o_dil': dense(keys[17], (DIL_HEADS_PER_GROUP * DIL_HEAD_DIM, D_MODEL)),
        'w_out': dense(keys[18], (D_MODEL, D_MODEL)),
        'g_post_mix': gain_vec(keys[19], D_MODEL),
        'g_pre_ff2': gain_vec(keys[20], D_MODEL),
        'w_gate2': dense(keys[21], (D_MODEL, D_FF)),
        'w_up2': dense(keys[22], (D_MODEL, D_FF)),
        'w_down2': dense(keys[23], (D_FF, D_MODEL)),
        'g_post_ff2': gain_vec(keys[24], D_MODEL),
    }

def reference(x, c, positions, w_ada, b_ada, g_pre_ff1, w_gate1, w_up1, w_down1, g_post_ff1,
              g_pre_mix, w_in, g_cq, w_uq, g_ckv, w_ukv, w_o_mla, w_o_dil, w_out, g_post_mix,
              g_pre_ff2, w_gate2, w_up2, w_down2, g_post_ff2):
    B = x.shape[0]
    cos_m, sin_m = rope_cos_sin(positions, MLA_ROPE, MLA_THETA)
    cos_p, sin_p = rope_cos_sin(positions, ROPE_PART, ROPE_THETA)
    cond = jax.nn.silu(c)
    for l in range(DEPTH):
        ada = (cond @ w_ada[l] + b_ada[l]).reshape(B, N_SUBLAYERS, N_MOD, D_MODEL)
        x = ffn_sublayer(x, ada[:, 0, 0], ada[:, 0, 1], ada[:, 0, 2],
                         g_pre_ff1[l], w_gate1[l], w_up1[l], w_down1[l], g_post_ff1[l])
        u = modulate(rms_norm(x, g_pre_mix[l]), ada[:, 1, 0], ada[:, 1, 1])
        y = token_mixer(u, cos_m, sin_m, cos_p, sin_p, w_in[l], g_cq[l], w_uq[l], g_ckv[l], w_ukv[l],
                        w_o_mla[l], w_o_dil[l], w_out[l])
        x = x + ada[:, 1, 2][:, None, :] * rms_norm(y, g_post_mix[l])
        x = ffn_sublayer(x, ada[:, 2, 0], ada[:, 2, 1], ada[:, 2, 2],
                         g_pre_ff2[l], w_gate2[l], w_up2[l], w_down2[l], g_post_ff2[l])
    return x


_drawn_inputs = setup_inputs


def setup_inputs(seed=0):
    import zlib

    import numpy as np

    out = dict(_drawn_inputs(seed))
    spreads = {}
    factors = {'g_post_ff1': 3.525, 'g_cq': 6.63, 'g_pre_ff2': 2.951, 'g_post_ff2': 3.625}
    for name, (base, spread) in spreads.items():
        noise = np.random.default_rng([zlib.crc32(name.encode()), seed]).standard_normal(out[name].shape)
        drawn = base * np.exp(spread * noise) if base else spread * noise
        out[name] = __import__('jax').numpy.asarray(drawn.astype(out[name].dtype))
    for name, factor in factors.items():
        out[name] = (out[name] * factor).astype(out[name].dtype)
    return out
```

```python
import math
from contextlib import ExitStack

import numpy as np

import concourse.bass as bass
from concourse import mybir

F32 = mybir.dt.float32
F32R = mybir.dt.float32r
I32 = mybir.dt.int32
ALU = mybir.AluOpType
ACT = mybir.ActivationFunctionType
AXIS = mybir.AxisListType

P = 128
EPS = 1e-6
MASKED = -1e30


class Steps:

    def __init__(self, engine, sem):
        self.engine, self.sem, self.n = engine, sem, 0

    def mark(self, instruction):
        self.n += 1
        return instruction.then_inc(self.sem, 1)

    def settle(self):
        self.engine.wait_ge(self.sem, self.n)


def encoder_block(nc, ins, out):
    D = ins["x"].shape[2]
    T = ins["x"].shape[1]
    FF = ins["w_gate1"].shape[2]
    KD, KT, KF = D // P, T // P, FF // P
    QL = ins["g_cq"].shape[1]
    KVL = ins["g_ckv"].shape[1]
    NOPE, ROPE, VD = 64, 32, 64
    HM = ins["w_uq"].shape[2] // (NOPE + ROPE)
    HE = NOPE + ROPE
    MLA_SCALE = float(HE) ** -0.5
    G, HG, E = 3, 4, 64
    GW = HG * E
    DIL_SCALE = float(E) ** -0.5
    RP = E // 4
    OFF_DIL = QL + KVL + ROPE
    OFF_GATE = OFF_DIL + 3 * G * GW
    LAT = OFF_DIL
    MM, MP = ROPE // 2, RP // 2
    DIL = 4
    assert (D, T, FF) == (1024, 512, 2816)

    N_GU1 = 0
    N_DN1 = N_GU1 + 2 * KF
    N_LAT = N_DN1 + 2 * KF
    N_KV = N_LAT + KD // 2
    N_UQ = N_KV + 1
    N_D0 = N_UQ + QL // P
    N_D12 = N_D0 + KD
    N_V12 = N_D12 + KD
    N_MRG = N_V12 + KD // 2
    MRG = 11
    N_OUT = N_MRG + 2 * MRG
    N_GU2 = N_OUT + 2 * KD
    N_DN2 = N_GU2 + 2 * KF
    N_END = N_DN2 + 2 * KF
    RING = 4
    LEAD = 2
    TOP_WORDS = 22264

    GU_BASE = (N_GU1, N_GU2)
    DN_BASE = (N_DN1, N_OUT, N_DN2)
    DN_CHUNKS = (KF, KD, KF)
    DN_COUNT = (0, 2 * KF, 2 * KF + 2 * KD)
    Y_BANK = ((0, 4), (4, 0), (0, 4))

    def y_bank(d, t):
        return Y_BANK[d][t // 2] + 2 * (t % 2)

    def x_bank(s, t):
        return (4, 6, 2, 0)[t] if s == 0 else y_bank(s - 1, t)

    w_gu = [[ins[n][0].rearrange("(k p) f -> p k f", p=P) for n in ("w_gate" + q, "w_up" + q)] for q in "12"]
    w_dn = [ins["w_down1"][0], ins["w_out"][0], ins["w_down2"][0]]
    w_in = ins["w_in"][0].rearrange("(k p) f -> p k f", p=P)
    w_ada = ins["w_ada"][0]

    with ExitStack() as ctx:
        def sem(name):
            return ctx.enter_context(nc.semaphore(name))

        def sb(scope, name, shape, dt=F32):
            return scope.enter_context(nc.sbuf_tensor(name, shape, dt))

        dil_nm = sb(ctx, "dil_nm", [P, 2, 2, KT, 2])
        dil_z = sb(ctx, "dil_z", [P, 2, 2, KT, 2])
        x = sb(ctx, "x_resid", [P, KT, D])
        w_raw = sb(ctx, "w_raw", [P, RING, 1024])
        w_hi = sb(ctx, "w_hi", [P, RING, 1024], F32R)
        w_lo = sb(ctx, "w_lo", [P, RING, 1024], F32R)
        h_hi = sb(ctx, "h_hi", [P, KD, T], F32R)
        h_lo = sb(ctx, "h_lo", [P, KD, T], F32R)
        ident = sb(ctx, "ident", [P, P])
        rows_a = sb(ctx, "rows_a", [P, P])
        rows_b = sb(ctx, "rows_b", [P, P])
        RA_B, RA_C, RA_G = 0, 9 * KD, 10 * KD
        RA_N = 13 * KD
        RB_GP, RB_CQ, RB_CKV = 0, 3 * KD, 3 * KD + QL // P
        RB_N = RB_CKV + 1
        col_a = sb(ctx, "col_a", [P, RA_N])
        col_b = sb(ctx, "col_b", [P, RB_N])
        cond = sb(ctx, "cond", [P, KD])
        ada_col = sb(ctx, "ada_col", [P, 9, KD])
        scale_col = sb(ctx, "scale_col", [P, 3, KD])
        gate_col = sb(ctx, "gate_col", [P, 3, KD])
        stat = sb(ctx, "stat", [P, 160])
        neg_half = sb(ctx, "neg_half", [P, 2])
        pos_i = sb(ctx, "pos_i", [P, KT], I32)
        pos_f = sb(ctx, "pos_f", [P, KT])
        inv_freq = sb(ctx, "inv_freq", [P, MM + MP])
        ang = sb(ctx, "ang", [P, 4, KT, MM + MP])
        cos_t = sb(ctx, "cos_t", [P, KT, MM + MP])
        sin_t = sb(ctx, "sin_t", [P, KT, MM + MP])
        mask0 = sb(ctx, "mask0", [P, 3, P])
        mask12 = sb(ctx, "mask12", [P, 2, P])
        residue = sb(ctx, "residue", [P, P])

        with ExitStack() as s:
            sb(s, "below_the_top", [P, TOP_WORDS])
            o_mla = sb(s, "o_mla", [P, HM // 2, T])
            u12 = sb(s, "u12", [P, 2, T])
            u0 = sb(s, "u0", [P, 2, T])

        with ExitStack() as s:
            q_nat = sb(s, "q_nat", [P, KT, HM * HE])
            c_hi = sb(s, "c_hi", [P, 3, T], F32R)
            c_lo = sb(s, "c_lo", [P, 3, T], F32R)
            ukv_hi = sb(s, "ukv_hi", [P, 1024], F32R)
            ukv_lo = sb(s, "ukv_lo", [P, 1024], F32R)
            mq_hi = sb(s, "mq_hi", [P, 2, T], F32R)
            mq_lo = sb(s, "mq_lo", [P, 2, T], F32R)
            mk_hi = sb(s, "mk_hi", [P, 2, T], F32R)
            mk_lo = sb(s, "mk_lo", [P, 2, T], F32R)
            mv_hi = sb(s, "mv_hi", [P, KT, HM * VD], F32R)
            mv_lo = sb(s, "mv_lo", [P, KT, HM * VD], F32R)
            with ExitStack() as s2:
                k_rot = sb(s2, "k_rot", [P, KT, HE])
                lat = sb(s2, "lat", [P, KT, LAT])
                c_t = sb(s2, "c_t", [P, 3, T])
                rot_m = sb(s2, "rot_m", [P, 4, KT * HM * MM])
            with ExitStack() as s2:
                mp = sb(s2, "mla_p", [P, 3, T])
                mpt_hi = sb(s2, "mla_pt_hi", [P, 2, KT, 256], F32R)
                mpt_lo = sb(s2, "mla_pt_lo", [P, 2, KT, 256], F32R)
        with ExitStack() as s:
            qk12 = sb(s, "qk12", [P, KT, 2, 2 * GW])
            dq_hi = sb(s, "dq_hi", [P, 2, T], F32R)
            dq_lo = sb(s, "dq_lo", [P, 2, T], F32R)
            kz_hi = sb(s, "kz_hi", [P, 2, 2, T], F32R)
            kz_lo = sb(s, "kz_lo", [P, 2, 2, T], F32R)
            dpt_hi = sb(s, "dpt_hi", [P, KT, T], F32R)
            dpt_lo = sb(s, "dpt_lo", [P, KT, T], F32R)
            dp = sb(s, "dil_p", [P, 3, T])
            rot_d = sb(s, "rot_d", [P, 4, 4 * HG * MP])
            with ExitStack() as s2:
                qk0 = sb(s2, "qk0", [P, KT, 2 * GW])
                v0_hi = sb(s2, "v0_hi", [P, KT, GW], F32R)
                v0_lo = sb(s2, "v0_lo", [P, KT, GW], F32R)
            with ExitStack() as s2:
                v12_hi = sb(s2, "v12_hi", [P, KT, 2 * GW], F32R)
                v12_lo = sb(s2, "v12_lo", [P, KT, 2 * GW], F32R)
        g_row = sb(ctx, "g_row", [P, D])
        with ExitStack() as s:
            junk = sb(s, "junk", [P, D])
            upd = sb(s, "upd", [P, D])
            xn = sb(s, "xn", [P, D])
            h32 = sb(s, "h32", [P, 2, KD, P])
            a_hi = sb(s, "a_hi", [P, RING, 256], F32R)
            a_lo = sb(s, "a_lo", [P, RING, 256], F32R)
            with ExitStack() as s2:
                a_buf = sb(s2, "a_buf", [P, KF * T])
                silu = sb(s2, "silu", [P, 2, T])
                ada_raw = sb(s2, "ada_raw", [P, 4, D])
                ada_acc = sb(s2, "ada_acc", [P, D])
            with ExitStack() as s2:
                m_t = sb(s2, "m_t", [P, KD * T])
                sg_a = sb(s2, "sg_a", [P, KT, T])
                sg_b = sb(s2, "sg_b", [P, KT, T])
                mix_max = sb(s2, "mix_max", [P, T])
                mix = sb(s2, "mix", [P, 2, 4, T])
        with ExitStack() as s:
            om_hi = sb(s, "om_hi", [P, HM // 2, T], F32R)
            om_lo = sb(s, "om_lo", [P, HM // 2, T], F32R)
            od_hi = sb(s, "od_hi", [P, 2, T], F32R)
            od_lo = sb(s, "od_lo", [P, 2, T], F32R)
        ps = ctx.enter_context(nc.psum_tensor("ps", [P, 8, 512], F32))

        st_y = stat[:, 0:12]
        st_yr = stat[:, 12:24]
        st_x = stat[:, 24:40]
        st_xr = stat[:, 40:56]
        st_eps = stat[:, 56:64]
        st_lat = stat[:, 64:72].rearrange("p (t c) -> p t c", c=2)
        st_latr = stat[:, 72:80].rearrange("p (t c) -> p t c", c=2)
        mla_nm = stat[:, 80:112]
        mla_z = stat[:, 112:144]

        x_in = [sem(f"x_in{t}") for t in range(KT)]
        rows_a_in = sem("rows_a_in")
        rows_b_in = sem("rows_b_in")
        pos_in = sem("pos_in")
        raw_in = [sem(f"raw_in{i}") for i in range(RING)]
        hi_ready = sem("hi_ready")
        lo_ready = sem("lo_ready")
        w_used = sem("w_used")
        start_in = [sem(f"start_in{i}") for i in range(2 * KD)]
        ada_in = [sem(f"ada_in{i}") for i in range(4)]
        ada_added = sem("ada_added")
        ada_turned = sem("ada_turned")
        ada_summed = sem("ada_summed")
        consts_ready = sem("consts_ready")
        masks_ready = sem("masks_ready")
        residue_ready = sem("residue_ready")
        rows_turned = sem("rows_turned")
        cols_ready = sem("cols_ready")
        cond_ready = sem("cond_ready")
        gates_ready = sem("gates_ready")
        sins_ready = sem("sins_ready")
        trig_ready = sem("trig_ready")
        g_spread = sem("g_spread")
        g_ready = sem("g_ready")
        silu_done = sem("silu_done")
        a_ready = sem("a_ready")
        a_hi_ready = sem("a_hi_ready")
        a_lo_ready = sem("a_lo_ready")
        y_squared = sem("y_squared")
        y_rms = sem("y_rms")
        x_new = sem("x_new")
        x_squared = sem("x_squared")
        x_rms = sem("x_rms")
        xn_ready = sem("xn_ready")
        third_summed = sem("third_summed")
        v12_half = sem("v12_half")
        x_turned = sem("x_turned")
        h32_ready = sem("h32_ready")
        h32_upper_ready = sem("h32_upper_ready")
        first_scale_ready = sem("first_scale_ready")
        h_hi_ready = sem("h_hi_ready")
        h_ready = sem("h_ready")
        lat_copied = sem("lat_copied")
        lat_squared = sem("lat_squared")
        lat_rms = sem("lat_rms")
        lat_normed = sem("lat_normed")
        lat_turned = sem("lat_turned")
        c_t_ready = sem("c_t_ready")
        c_hi_ready = sem("c_hi_ready")
        c_ready = sem("c_ready")
        krot_hi = sem("krot_hi")
        krot_turned = sem("krot_turned")
        residue_mult = sem("residue_mult")
        krot_ready = sem("krot_ready")
        mv_done = sem("mv_done")
        mv_hi_ready = sem("mv_hi_ready")
        mv_ready = sem("mv_ready")
        uq_done = sem("uq_done")
        lat_half = sem("lat_half")
        m_pv = sem("m_pv")
        pv12_used = sem("pv12_used")
        mix_wide = sem("mix_wide")
        stats_ready = sem("stats_ready")
        q_copied = sem("q_copied")
        q_rotated = sem("q_rotated")
        m_turned = sem("m_turned")
        m_qk_hi = sem("m_qk_hi")
        m_qk_ready = sem("m_qk_ready")
        m_scores = sem("m_scores")
        m_max = sem("m_max")
        m_exp = sem("m_exp")
        m_normed = sem("m_normed")
        m_pt_done = sem("m_pt_done")
        m_pt_hi = sem("m_pt_hi")
        m_pt_ready = sem("m_pt_ready")
        m_out_copied = sem("m_out_copied")
        d0_copied = sem("d0_copied")
        v0_hi_ready = sem("v0_hi_ready")
        v0_ready = sem("v0_ready")
        d0_rotated = sem("d0_rotated")
        d12_copied = sem("d12_copied")
        d12_rotated = sem("d12_rotated")
        v12_hi_ready = sem("v12_hi_ready")
        v12_ready = sem("v12_ready")
        kz_clear = sem("kz_clear")
        d_turned = sem("d_turned")
        d_qk_hi = sem("d_qk_hi")
        d_qk_ready = sem("d_qk_ready")
        d_scores = sem("d_scores")
        d_max = sem("d_max")
        d_exp = sem("d_exp")
        d_pt_done = sem("d_pt_done")
        d_pt_hi = sem("d_pt_hi")
        d_pt_ready = sem("d_pt_ready")
        pv0_used = sem("pv0_used")
        u_copied = sem("u_copied")
        mix_spread = sem("mix_spread")
        mix_copied = sem("mix_copied")
        mix_diff = sem("mix_diff")
        mix_exp = sem("mix_exp")
        mixed = sem("mixed")
        om_hi_ready = sem("om_hi_ready")
        om_ready = sem("om_ready")
        od_hi_ready = sem("od_hi_ready")
        od_ready = sem("od_ready")
        ga_ready = sem("ga_ready")
        gb_ready = sem("gb_ready")
        om_added = sem("om_added")
        merged = sem("merged")
        m_t_done = sem("m_t_done")
        m_t_ready = sem("m_t_ready")
        act_own = sem("act_own")
        dve_own = sem("dve_own")
        pool_own = sem("pool_own")
        out_written = sem("out_written")

        MU = HM * KT
        D_UNITS = [("local", p, a, t) for p in range(2) for a in range(2) for t in range(KT)] \
            + [("strided", p, 0, r) for p in range(2) for r in range(KT)]
        N_LOCAL = 4 * KT

        def chunks(t):
            return range(max(0, t - 1), min(KT, t + 2))

        def pv0_steps(t):
            return [] if t == 0 else [t - 1] if t < KT - 1 else [t - 1, t]

        PREP = [("local", 0, 0, 0, 0), ("local", 1, 1, 0, 0), ("strided", 0, 0, 4, 8), ("strided", 1, 0, 6, 16),
                ("strided", 0, 1, 0, 20), ("strided", 1, 1, 0, 20)]
        STAGED = KF * T // D
        M_BANKS = ((0, 4, 0, 4), (4, 0, 4, 0))
        G_BANK = (2, 0, 2)

        def w_shape(n):
            if N_LAT <= n < N_KV:
                return 2 * LAT
            if N_UQ <= n < N_D12:
                return 768
            return 1024

        def pt_view(buf, v):
            kind, _, _, t = D_UNITS[v]
            if kind == "local":
                c = chunks(t)
                return buf[:, c[0]:c[-1] + 1, t * P:(t + 1) * P]
            return buf[:, v % KT, :]

        def pt_bank(v):
            kind, _, _, t = D_UNITS[v]
            if kind == "local":
                return ps[:, 5 + v % 2, 0:len(chunks(t)) * P].rearrange("p (c n) -> p c n", n=P)
            return ps[:, 5 + v % 2, :]

        def pt_free(v):
            if v < N_LOCAL:
                h, t = v // KT, v % KT
                return pv0_used, max(0, KT * (h - 1) + min(t + 2, KT)) if h else 0
            return (pv0_used, N_LOCAL) if v < N_LOCAL + KT else (pv12_used, v - N_LOCAL - KT + 1)

        def start_slot(j):
            return a_buf[:, j * D:(j + 1) * D] if j < STAGED else ada_raw[:, j % 4, :]

        block = ctx.enter_context(nc.Block())

        @block.sync
        def _(sp):
            def slot_free(n):
                sp.wait_ge(lo_ready, n - RING + 1)

            def load(static_n, dst, src):
                sp.dma_start(dst, src).then_inc(raw_in[static_n % RING], 16)

            def load_tile(g, i, q, first=False):
                for m in range(2):
                    s_n = GU_BASE[g] + 2 * q + m
                    if not first:
                        slot_free(i * 4 + s_n)
                    dst = w_raw[:, s_n % RING, :].rearrange("p (k f) -> p k f", k=KD)
                    load(s_n, dst, w_gu[g][m][:, :, bass.ds(i * (2 * P) + q * P, P)])

            def load_ada(v, k):
                sp.wait_ge(ada_added, v * KD + (k - 3))
                sp.dma_start(ada_raw[:, k % 4, :], w_ada[k * P:(k + 1) * P, bass.ds(v * D, D)])\
                    .then_inc(ada_in[k % 4], 16)

            def row(dst, name, a, n, signal):
                sp.dma_start(dst[a:a + n, :], ins[name][0].rearrange("(r e) -> r e", e=P)).then_inc(signal, 16)

            def load_start(j):
                if j >= STAGED + 4:
                    sp.wait_ge(ada_added, j - 3)
                v, k = j // KD, j % KD
                sp.dma_start(start_slot(j), w_ada[k * P:(k + 1) * P, v * D:(v + 1) * D]).then_inc(start_in[j], 16)

            def load_x(t):
                sp.dma_start(x[:, t, :], ins["x"][0, t * P:(t + 1) * P, :]).then_inc(x_in[t], 16)

            row(rows_a, "c", RA_C, KD, rows_a_in)
            row(rows_a, "b_ada", RA_B, 9 * KD, rows_a_in)
            for s, name in enumerate(("g_pre_ff1", "g_pre_mix", "g_pre_ff2")):
                row(rows_a, name, RA_G + s * KD, KD, rows_a_in)
            load_start(0)
            load_x(0)
            load_start(1)
            load_x(1)
            for s, name in enumerate(("g_post_ff1", "g_post_mix", "g_post_ff2")):
                row(rows_b, name, RB_GP + s * KD, KD, rows_b_in)
            row(rows_b, "g_cq", RB_CQ, QL // P, rows_b_in)
            row(rows_b, "g_ckv", RB_CKV, 1, rows_b_in)
            load_start(2)
            load_x(2)
            load_start(3)
            load_x(3)
            for j in range(4, 10):
                load_start(j)
            load_tile(0, 0, 0, first=True)
            for j in range(10, 2 * KD):
                load_start(j)
            sp.dma_start(pos_i[:, :], ins["positions"][0].rearrange("(t p) -> p t", p=P),
                         allow_slow_non_contiguous=True).then_inc(pos_in, 16)
            load_tile(0, 0, 1, first=True)
            load_tile(0, 1, 0)
            with sp.Fori(1, 8) as i:
                load_tile(0, i, 1)
                for k in range(4):
                    load_ada(i + 1, k)
                load_tile(0, i + 1, 0)
                for k in range(4, KD):
                    load_ada(i + 1, k)
            with sp.Fori(8, KF // 2 - 1) as i:
                load_tile(0, i, 1)
                load_tile(0, i + 1, 0)
            load_tile(0, KF // 2 - 1, 1)

            def load_dn(d):
                n0, nch = DN_BASE[d], DN_CHUNKS[d]
                for hf in range(2):
                    base = n0 + hf * nch
                    with sp.Fori(0, nch // 4) as i:
                        for j in range(4):
                            slot_free(i * 4 + (base + j))
                            load(base + j, w_raw[:, (base + j) % RING, :],
                                 w_dn[d][bass.ds(i * (4 * P) + j * P, P), :])
                    for c in range(nch // 4 * 4, nch):
                        slot_free(base + c)
                        load(base + c, w_raw[:, (base + c) % RING, :], w_dn[d][c * P:(c + 1) * P, :])

            load_dn(0)
            for b in range(KD // 2):
                n = N_LAT + b
                slot_free(n)
                load(n, w_raw[:, n % RING, 0:2 * LAT].rearrange("p (k f) -> p k f", k=2),
                     w_in[:, 2 * b:2 * b + 2, 0:LAT])
            slot_free(N_KV)
            load(N_KV, w_raw[:, N_KV % RING, :], ins["w_ukv"][0])
            for b in range(QL // P):
                n = N_UQ + b
                slot_free(n)
                load(n, w_raw[:, n % RING, 0:HM * HE], ins["w_uq"][0, b * P:(b + 1) * P, :])
            dil = w_in[:, :, OFF_DIL:OFF_GATE].rearrange("p k (m g e) -> p k m g e", m=3, g=G)
            for k in range(KD):
                n = N_D0 + k
                slot_free(n)
                load(n, w_raw[:, n % RING, 0:3 * GW].rearrange("p (m e) -> p m e", m=3), dil[:, k, :, 0, :])
            for k in range(KD):
                n = N_D12 + k
                slot_free(n)
                load(n, w_raw[:, n % RING, :].rearrange("p (m e) -> p m e", m=2),
                     w_in[:, k, OFF_DIL + GW:OFF_DIL + 7 * GW].rearrange("p (m e) -> p m e", m=2)[:, :, 0:2 * GW])
            for b in range(KD // 2):
                n = N_V12 + b
                slot_free(n)
                load(n, w_raw[:, n % RING, :].rearrange("p (k f) -> p k f", k=2),
                     w_in[:, 2 * b:2 * b + 2, OFF_DIL + 7 * GW:OFF_GATE])
            for hf in range(2):
                n = N_MRG + hf * MRG
                cols = slice(hf * T, (hf + 1) * T)
                srcs = [w_in[:, 2 * b:2 * b + 2, OFF_GATE + m * D + hf * T:OFF_GATE + m * D + (hf + 1) * T]
                        for m in range(2) for b in range(KD // 2)]
                srcs += [ins["w_o_mla"][0, 2 * b * P:(2 * b + 2) * P, cols].rearrange("(k p) f -> p k f", p=P)
                         for b in range(2)]
                srcs += [ins["w_o_dil"][0, :, cols].rearrange("(k p) f -> p k f", p=P)]
                for src in srcs:
                    slot_free(n)
                    load(n, w_raw[:, n % RING, :].rearrange("p (k f) -> p k f", k=2), src)
                    n += 1
            load_dn(1)
            with sp.Fori(0, KF // 2) as i:
                load_tile(1, i, 0)
                load_tile(1, i, 1)
            load_dn(2)
            for t in range(KT):
                sp.wait_ge(x_new, 8 + t + 1)
                sp.dma_start(out[0, t * P:(t + 1) * P, :], x[:, t, :]).then_inc(out_written, 16)
            sp.wait_ge(out_written, 16 * KT)

        @block.gpsimd
        def _(pool):
            own = Steps(pool, pool_own)
            own.mark(pool.memset(ident[:, :], 0.0))
            own.mark(pool.memset(residue[:, :], 0.0))
            own.mark(pool.memset(mask0[:, :, :], 0.0))
            own.mark(pool.memset(mask12[:, :, :], 0.0))
            own.mark(pool.memset(neg_half[:, :], -0.5))
            for base, n, dim, theta in ((0, MM, ROPE, 10000.0), (MM, MP, RP, 500000.0)):
                for j in range(n):
                    f = np.float32(theta) ** (-np.float32(2 * j) / np.float32(dim))
                    own.mark(pool.memset(inv_freq[:, base + j:base + j + 1], float(f)))
            own.settle()
            pool.affine_select(out=ident[:, :], in_=ident[:, :], compare_op=ALU.not_equal, fill=1.0,
                               base=0, pattern=[[-1, P]], channel_multiplier=1).then_inc(consts_ready, 1)

            last = []

            def rms(n, src, dst, signal, count):
                if last:
                    pool.wait_ge(*last)
                own.mark(pool.tensor_scalar(st_eps[:, 0:n], src, EPS, None, ALU.add))
                own.settle()
                pool.tensor_tensor(dst, st_eps[:, 0:n], neg_half[:, 0:n], ALU.pow).then_inc(signal, 1)
                last[:] = [signal, count]

            def rms_y(m):
                pool.wait_ge(y_squared, m + 1)
                rms(1, st_y[:, m:m + 1], st_yr[:, m:m + 1], y_rms, m + 1)

            def rms_x(m):
                pool.wait_ge(x_squared, m + 1)
                rms(1, st_x[:, m:m + 1], st_xr[:, m:m + 1], x_rms, m + 1)

            for t in range(KT):
                rms_x(t)
            own.settle()
            own.mark(pool.affine_select(
                out=residue[0:DIL, :].rearrange("p (m a) -> p m a", a=DIL),
                in_=residue[0:DIL, :].rearrange("p (m a) -> p m a", a=DIL), compare_op=ALU.not_equal,
                fill=1.0, base=0, pattern=[[0, P // DIL], [-1, DIL]], channel_multiplier=1))
            own.settle()
            pool.memset(st_eps[:, 7:8], 0.0).then_inc(residue_ready, 1)
            for m, pat, base in ((mask0[:, :, :], [[P, 3], [1, P]], -P), (mask12[:, 0, :], [[1, P]], 0)):
                own.mark(pool.affine_select(out=m, in_=m, compare_op=ALU.is_ge, fill=MASKED,
                                            base=base + E, pattern=pat, channel_multiplier=-1))
                own.settle()
                own.mark(pool.affine_select(out=m, in_=m, compare_op=ALU.is_ge, fill=MASKED, base=E - base,
                                            pattern=[[-a, b] for a, b in pat], channel_multiplier=1))
                own.settle()
            pool.memset(st_eps[:, 6:7], 0.0).then_inc(masks_ready, 1)

            def post(d, tiles):
                for t in tiles:
                    rms_y(4 * d + t)
                if d < 2:
                    for t in tiles:
                        rms_x(4 * (d + 1) + t)

            post(0, (0, 1))
            post(0, (2, 3))
            for t in range(KT):
                pool.wait_ge(lat_squared, 2 * (t + 1))
                rms(2, st_lat[:, t, :], st_latr[:, t, :], lat_rms, t + 1)
            pool.wait_ge(w_used, N_D0 + 1)
            for z in (kz_hi, kz_lo):
                for a in range(2):
                    pool.memset(z[(1 - a) * E:(1 - a) * E + E, :, a, :].bitcast(F32), 0.0).then_inc(kz_clear, 1)
            post(1, (0, 1))
            post(1, (2, 3))
            post(2, (0, 1))
            post(2, (2, 3))

        @block.scalar
        def _(act):
            own = Steps(act, act_own)
            copy, square = ACT.Copy, ACT.Square
            split = [0]
            junk_last = []

            def split_block(n, s_n):
                slot = s_n % RING
                act.wait_ge(raw_in[slot], n * 4 + (16 - 4 * slot))
                if s_n >= RING:
                    act.wait_ge(w_used, n - (RING - 1))
                width = w_shape(s_n)
                dst = ukv_hi[:, :] if s_n == N_KV else w_hi[:, slot, 0:width]
                act.activation(dst, w_raw[:, slot, 0:width], copy).then_inc(hi_ready, 1)

            def split_to(n):
                while split[0] <= min(n, N_END - 1):
                    split_block(split[0], split[0])
                    split[0] += 1

            def split_a(d, hf, c, s_c):
                src = m_t if d == 1 else a_buf
                slot = (hf * DN_CHUNKS[d] + s_c) % RING
                if hf or s_c >= RING:
                    act.wait_ge(w_used, c + (DN_BASE[d] + hf * DN_CHUNKS[d] - RING + 1))
                if d == 1:
                    act.wait_ge(m_t_ready, c + 1)
                act.activation(a_hi[:, slot, :], src[:, bass.ds(c * T + hf * 256, 256)], copy)\
                    .then_inc(a_hi_ready, 1)

            def squares(src, dst, signal, count):
                if junk_last:
                    act.wait_ge(*junk_last)
                act.activation(junk[:, :], src, square, scale=float(D) ** -0.5, accum_out=dst).then_inc(signal, 1)
                junk_last[:] = [signal, count]

            def sq_y(m):
                d, t = m // 4, m % 4
                if t == 2:
                    act.wait_ge(third_summed, d + 1)
                else:
                    act.wait_ge(w_used, DN_BASE[d] + (t // 2 + 1) * DN_CHUNKS[d])
                b = y_bank(d, t)
                squares(ps[:, b:b + 2, :].rearrange("p a b -> p (a b)"), st_y[:, m:m + 1], y_squared, m + 1)

            def sq_x(m):
                s, t = m // 4, m % 4
                if s:
                    act.wait_ge(x_new, m - 4 + 1)
                else:
                    act.wait_ge(x_in[t], 16)
                squares(x[:, t, :], st_x[:, m:m + 1], x_squared, m + 1)

            def modulated_upper(m):
                s, t = m // 4, m % 4
                act.wait_ge(x_turned, m + 1)
                if s == 0:
                    act.wait_ge(first_scale_ready, 1)
                if m >= 2:
                    act.wait_ge(h_hi_ready, m - 1)
                    act.wait_ge(h_ready, m - 1)
                for c in range(KD // 2, KD):
                    i = act.activation(h32[:, m % 2, c, :], ps[:, x_bank(s, t) + 1, c % 4 * P:(c % 4 + 1) * P],
                                       ACT.Identity, scale=scale_col[:, s, c:c + 1], bias=ada_col[:, 3 * s, c:c + 1])
                i.then_inc(h32_upper_ready, 1)

            def h_high(m):
                t = m % 4
                act.wait_ge(h32_ready, m + 1)
                act.wait_ge(h32_upper_ready, m + 1)
                act.activation(h_hi[:, :, t * P:(t + 1) * P], h32[:, m % 2, :, :], copy).then_inc(h_hi_ready, 1)

            def gain_row(s):
                act.wait_ge(g_spread, s + 1)
                b = G_BANK[s]
                act.activation(g_row[:, :], ps[:, b:b + 2, :].rearrange("p a b -> p (a b)"), copy)\
                    .then_inc(g_ready, 1)

            def gate_up(g):
                n0, f0 = GU_BASE[g], KF * g

                def tile(i, q, straight):
                    n = n0 + 2 * q + 2
                    if straight:
                        split_to(n + 4 * i + 1)
                    else:
                        split_block(i * 4 + n, n + 4)
                        split_block(i * 4 + (n + 1), n + 5)
                    act.wait_ge(w_used, i * 4 + (n0 + 2 * q + 2))
                    if not (straight and i == 0):
                        act.wait_ge(a_ready, i * 2 + (f0 + q - 1))
                    act.activation(silu[:, q, :], ps[:, 4 + 2 * q, :], ACT.Silu).then_inc(silu_done, 1)

                for q in range(2):
                    tile(0, q, True)
                for lo, hi in ((1, 8), (8, KF // 2)):
                    with act.Fori(lo, hi) as i:
                        for q in range(2):
                            tile(i, q, False)
                    if lo == 1:
                        gain_row(2 * g)
                split[0] = n0 + 2 * KF + LEAD

            def down_chunk(d, hf, c):
                nch = DN_CHUNKS[d]
                split_to(DN_BASE[d] + hf * nch + c + LEAD)
                if c + LEAD < nch:
                    split_a(d, hf, c + LEAD, c + LEAD)
                elif hf == 0:
                    split_a(d, 1, c + LEAD - nch, c + LEAD - nch)

            def down(d):
                nch, n0 = DN_CHUNKS[d], DN_BASE[d]

                def chunk_loop(hf, first, last):
                    base = n0 + hf * nch
                    with act.Fori(0, (last - first) // 4) as i:
                        for j in range(first, first + 4):
                            split_block(i * 4 + (base + j + LEAD), base + j + LEAD)
                            split_a(d, hf, i * 4 + (j + LEAD), j + LEAD)
                    split[0] = base + last + LEAD

                if nch > 8:
                    act.wait_ge(a_ready, KF * (1 + d // 2))
                    for c in range(LEAD):
                        split_a(d, 0, c, c)
                    for c in range(4):
                        down_chunk(d, 0, c)
                    chunk_loop(0, 4, 20)
                    down_chunk(d, 0, 20)
                    down_chunk(d, 0, 21)
                else:
                    for c in range(2, nch):
                        down_chunk(d, 0, c)
                        if c == 4:
                            gain_row(1)
                m = 4 * (d + 1)
                for c in range(8):
                    down_chunk(d, 1, c)
                    if c == 0:
                        sq_y(4 * d)
                        sq_y(4 * d + 1)
                    if d < 2 and c == 2:
                        sq_x(m)
                    if d < 2 and c == 3:
                        sq_x(m + 1)
                    if d < 2 and c == 5:
                        modulated_upper(m)
                    if d < 2 and c == 6:
                        modulated_upper(m + 1)
                        h_high(m)
                    if d < 2 and c == 7:
                        h_high(m + 1)
                if nch > 8:
                    chunk_loop(1, 8, 20)
                    down_chunk(d, 1, 20)
                    down_chunk(d, 1, 21)
                sq_y(4 * d + 2)
                sq_y(4 * d + 3)
                split_to(n0 + 2 * nch + 2)
                if d < 2:
                    sq_x(m + 2)
                split_to(n0 + 2 * nch + 3)
                if d < 2:
                    sq_x(m + 3)
                    for t in (2, 3):
                        modulated_upper(m + t)
                    for t in (2, 3):
                        h_high(m + t)

            act.wait_ge(rows_turned, 1)
            act.activation(col_a[:, :], ps[:, 0, 0:RA_N], copy).then_inc(cols_ready, 1)
            act.wait_ge(cols_ready, 1)
            act.activation(cond[:, :], col_a[:, RA_C:RA_C + KD], ACT.Silu).then_inc(cond_ready, 1)
            for t in range(KT):
                sq_x(t)
            act.wait_ge(rows_turned, 2)
            act.activation(col_b[:, :], ps[:, 1, 0:RB_N], copy).then_inc(cols_ready, 1)
            split_to(1)
            for t in (0, 2):
                modulated_upper(t)
                modulated_upper(t + 1)
                h_high(t)
                h_high(t + 1)
                split_to(3)
            act.wait_ge(sins_ready, 1)
            act.activation(sin_t[:, :, :], ang[:, 1, :, :], ACT.Sin).then_inc(trig_ready, 1)
            act.activation(cos_t[:, :, :], ang[:, 2, :, :], ACT.Sin).then_inc(trig_ready, 1)
            gate_up(0)
            down(0)

            rot_flat = rot_m[:, :, :].rearrange("p a b -> p (a b)")

            def lat_evac(t):
                if t < 2:
                    act.wait_ge(lat_half, 1)
                else:
                    act.wait_ge(w_used, N_LAT + KD // 2)
                act.activation(lat[:, t, :], ps[:, t, 0:LAT], copy).then_inc(lat_copied, 1)


            for half in range(2):
                for t in (2 * half, 2 * half + 1):
                    lat_evac(t)
                for t in (2 * half, 2 * half + 1):
                    act.wait_ge(lat_copied, t + 1)
                    for c, (a, b) in enumerate(((0, QL), (QL, QL + KVL))):
                        act.activation(rot_flat[:, (2 * t + c) * QL:(2 * t + c) * QL + b - a], lat[:, t, a:b], square,
                                       scale=float(b - a) ** -0.5, accum_out=st_lat[:, t, c:c + 1])\
                            .then_inc(lat_squared, 1)
                split_to(N_KV + 2 * half + 1)
            act.wait_ge(lat_turned, KT)
            act.wait_ge(c_t_ready, KT)
            for z in range(2):
                act.activation(mk_hi[NOPE:HE, z, :].rearrange("p (t n) -> p t n", t=KT),
                               ps[NOPE:HE, 4:8, 3 * P:4 * P], copy).then_inc(krot_hi, 1)
            act.activation(c_hi[:, :, :], c_t[:, :, :], copy).then_inc(c_hi_ready, 1)
            for t in range(KT):
                if t < KT - 1:
                    act.wait_ge(mv_done, t + 1)
                else:
                    act.wait_ge(w_used, N_KV + 1)
                act.activation(mv_hi[:, t, :], ps[:, 4 + t, :], copy).then_inc(mv_hi_ready, 1)
            for t in range(KT):
                if t < KT - 1:
                    act.wait_ge(uq_done, t + 1)
                else:
                    act.wait_ge(w_used, N_UQ + 2)
                act.activation(q_nat[:, t, :].rearrange("p (a b) -> p a b", a=2), ps[:, 2 * t:2 * t + 2, 0:384],
                               copy).then_inc(q_copied, 1)
            split_to(N_D0 + 3)

            def m_operands(h):
                z = h % 2
                act.wait_ge(m_turned, h + 1)
                if h >= 2:
                    act.wait_ge(m_scores, KT * (h - 1))
                act.activation(mq_hi[0:HE, z, :], ps[0:HE, 0, :], copy, scale=MLA_SCALE).then_inc(m_qk_hi, 1)
                act.activation(mk_hi[0:NOPE, z, :], ps[0:NOPE, 1, :], copy).then_inc(m_qk_hi, 1)

            def m_out_copy(h):
                act.wait_ge(m_pv, 2 * h + 2)
                a = h % 2 * VD
                act.activation(o_mla[a:a + VD, h // 2, :], ps[a:a + VD, 7, :], copy).then_inc(m_out_copied, 1)

            m_operands(0)
            for u in range(MU + 4):
                v = u - 3
                if 0 <= v < MU:
                    act.wait_ge(m_pt_done, v + 1)
                    if v >= 4:
                        act.wait_ge(m_pv, v // 2 - 1)
                    act.activation(mpt_hi[:, v // 2 % 2, :, v % 2 * P:v % 2 * P + P],
                                   ps[:, 5 + v % 2, :].rearrange("p (c n) -> p c n", c=KT), copy)\
                        .then_inc(m_pt_hi, 1)
                if u < MU:
                    act.wait_ge(m_max, u + 1)
                    if u >= 3:
                        act.wait_ge(m_pt_done, u - 2)
                    act.activation(mp[:, u % 3, :], ps[:, 2 + u % 3, :], ACT.Exp, bias=mla_nm[:, u:u + 1],
                                   accum_out=mla_z[:, u:u + 1]).then_inc(m_exp, 1)
                if u % KT == 1 and u // KT + 1 < HM:
                    m_operands(u // KT + 1)
                if u >= 8 and u % KT == 0:
                    m_out_copy(u // KT - 2)
            m_out_copy(HM - 1)

            split_to(N_D0 + 10)
            act.wait_ge(w_used, N_D0 + KD)
            for t in range(KT):
                act.activation(qk0[:, t, :], ps[:, 2 * t, :], copy).then_inc(d0_copied, 1)
                act.activation(v0_hi[:, t, :], ps[:, 2 * t + 1, 0:GW], copy).then_inc(v0_hi_ready, 1)
            split_to(N_V12 + 2)
            act.wait_ge(w_used, N_D12 + KD)
            for t in range(KT):
                act.activation(qk12[:, t, :, :], ps[:, 2 * t:2 * t + 2, :], copy).then_inc(d12_copied, 1)
            split_to(N_V12 + 3)

            def d_operands(i):
                kind, g, _, bank, before = PREP[i]
                act.wait_ge(d_turned, i + 1)
                if before:
                    act.wait_ge(d_scores, before)
                if i == 0:
                    act.wait_ge(kz_clear, 4)
                parts = [(dq_hi[:, g, :], ps[:, bank, :], DIL_SCALE)]
                parts += [(kz_hi[a * E:a * E + E, g, a, :], ps[a * E:a * E + E, bank + 1, :], 1.0) for a in range(2)]
                for dst, src, scale in parts:
                    if kind == "strided":
                        dst = dst.rearrange("p (r l) -> p r l", r=DIL)
                        src = src.rearrange("p (l r) -> p r l", r=DIL)
                    act.activation(dst, src, copy, scale=scale).then_inc(d_qk_hi, 1)

            def d_exp_unit(v):
                kind, p, a, t = D_UNITS[v]
                s = v % 3
                act.wait_ge(d_max, v + 1)
                if kind == "local":
                    w = len(chunks(t)) * P
                    act.activation(dp[:, s, 0:w], dp[:, s, 0:w], ACT.Exp, bias=dil_nm[:, 0, p, t, a:a + 1],
                                   accum_out=dil_z[:, 0, p, t, a:a + 1]).then_inc(d_exp, 1)
                else:
                    view = dp[:, s, :].rearrange("p (g a n) -> p a g n", g=2, a=2)
                    for b in range(2):
                        act.activation(view[:, b, :, :], view[:, b, :, :], ACT.Exp,
                                       bias=dil_nm[:, 1, p, t, b:b + 1],
                                       accum_out=dil_z[:, 1, p, t, b:b + 1]).then_inc(d_exp, 1)

            def d_pt_high(v):
                act.wait_ge(d_pt_done, v + 1)
                sem_, value = pt_free(v)
                if value:
                    act.wait_ge(sem_, value)
                act.activation(pt_view(dpt_hi, v), pt_bank(v), copy).then_inc(d_pt_hi, 1)

            def u_copy(i):
                if i < 4:
                    act.wait_ge(pv0_used, KT * (i + 1))
                    p, a = i // 2, i % 2
                    act.activation(u0[a * E:a * E + E, p, :], ps[a * E:a * E + E, 7, :], copy).then_inc(u_copied, 1)
                    return
                act.wait_ge(pv12_used, i - 3)
                p, r = (i - 4) // KT, (i - 4) % KT
                for a in range(2):
                    c = r % 2 * 256 + a * P
                    o = u12[a * E:a * E + E, p, :].rearrange("p (l r) -> p r l", r=DIL)[:, r, :]
                    act.activation(o, ps[a * E:a * E + E, 7, c:c + P], copy).then_inc(u_copied, 1)

            d_operands(0)
            for v in range(N_LOCAL + 4):
                if v == 2:
                    d_operands(1)
                if 0 <= v - 3 < N_LOCAL:
                    d_pt_high(v - 3)
                if v < N_LOCAL:
                    d_exp_unit(v)
                if v >= 8 and v % KT == 0:
                    u_copy(v // KT - 2)
            u_copy(3)
            d_operands(2)
            d_operands(3)
            split_to(N_MRG + 2)
            act.wait_ge(w_used, N_V12 + 4)
            for t in range(KT):
                act.activation(v12_hi[:, t, :], ps[:, t, :], copy).then_inc(v12_hi_ready, 1)
            split_to(N_MRG + 3)
            for v in range(N_LOCAL, len(D_UNITS) + 4):
                if v == 20:
                    d_operands(4)
                    d_operands(5)
                if N_LOCAL <= v - 3 < len(D_UNITS):
                    d_pt_high(v - 3)
                if v < len(D_UNITS):
                    d_exp_unit(v)
                if N_LOCAL <= v - 4 < len(D_UNITS):
                    u_copy(v - 4 - N_LOCAL + 4)

            for p in range(2):
                act.wait_ge(mix_spread, p + 1)
                for j in range(4):
                    o, i_ = mix[:, p, j, :], ps[:, 4 * p + j, :]
                    if j >= 2:
                        o = o.rearrange("p (l r) -> p r l", r=DIL)
                        i_ = i_.rearrange("p (r l) -> p r l", r=DIL)
                    act.activation(o, i_, copy).then_inc(mix_copied, 1)
            act.activation(om_hi[:, :, :], o_mla[:, :, :], copy).then_inc(om_hi_ready, 1)

            def merged_copy(hf):
                for c in range(4):
                    act.wait_ge(m_t_done, 4 * hf + c + 1)
                    act.activation(m_t[:, (4 * hf + c) * T:(4 * hf + c + 1) * T], ps[:, c, :], copy)\
                        .then_inc(m_t_ready, 1)

            for hf in range(2):
                n = N_MRG + hf * MRG
                ga, gb, om, od = M_BANKS[hf]
                if hf == 0:
                    split_to(n + 6)
                    for p in range(2):
                        for j in range(2):
                            act.wait_ge(mix_diff, 2 * p + j + 1)
                            act.activation(mix[:, p, 2 * j, :], mix[:, p, 2 * j, :], ACT.Exp).then_inc(mix_exp, 1)
                else:
                    split_to(n + 4)
                    merged_copy(0)
                split_to(n + 7)
                act.wait_ge(w_used, n + 4)
                if hf:
                    act.wait_ge(m_t_done, 4)
                for t in range(KT):
                    act.activation(sg_a[:, t, :], ps[:, ga + t, :], ACT.Sigmoid).then_inc(ga_ready, 1)
                split_to(n + 10)
                act.wait_ge(w_used, n + 8)
                for t in range(KT):
                    act.activation(sg_b[:, t, :], ps[:, gb + t, :], ACT.Sigmoid).then_inc(gb_ready, 1)
                split_to(n + 13)
                if hf == 0:
                    act.wait_ge(mixed, 2)
                    act.activation(od_hi[:, :, :], u12[:, :, :], copy).then_inc(od_hi_ready, 1)
                split_to(n + 14)
            for c in range(LEAD):
                split_a(1, 0, c, c)
            down_chunk(1, 0, 0)
            down_chunk(1, 0, 1)
            merged_copy(1)
            down(1)
            gate_up(1)
            down(2)

        @block.vector
        def _(dve):
            own = Steps(dve, dve_own)
            split = [0]

            def split_block(n, s_n):
                slot = s_n % RING
                dve.wait_ge(hi_ready, n + 1)
                width = w_shape(s_n)
                hi, lo = (ukv_hi[:, :], ukv_lo[:, :]) if s_n == N_KV else \
                    (w_hi[:, slot, 0:width], w_lo[:, slot, 0:width])
                dve.tensor_tensor(lo, w_raw[:, slot, 0:width], hi.bitcast(F32), ALU.subtract).then_inc(lo_ready, 1)

            def split_to(n):
                while split[0] <= min(n, N_END - 1):
                    split_block(split[0], split[0])
                    split[0] += 1

            def split_a(d, hf, c, s_c):
                src = m_t if d == 1 else a_buf
                slot = (hf * DN_CHUNKS[d] + s_c) % RING
                dve.wait_ge(a_hi_ready, c + (DN_COUNT[d] + hf * DN_CHUNKS[d] + 1))
                dve.tensor_tensor(a_lo[:, slot, :], src[:, bass.ds(c * T + hf * 256, 256)],
                                  a_hi[:, slot, :].bitcast(F32), ALU.subtract).then_inc(a_lo_ready, 1)

            def update(m):
                d, t = m // 4, m % 4
                dve.wait_ge(y_rms, m + 1)
                dve.wait_ge(g_ready, d + 1)
                if m:
                    dve.wait_ge(x_new, m)
                b = y_bank(d, t)
                own.mark(dve.scalar_tensor_tensor(upd[:, :], ps[:, b:b + 2, :].rearrange("p a b -> p (a b)"),
                                                  st_yr[:, m:m + 1], g_row[:, :], ALU.mult, ALU.mult))
                own.settle()
                dve.tensor_tensor(x[:, t, :], x[:, t, :], upd[:, :], ALU.add).then_inc(x_new, 1)

            def norm(m):
                dve.wait_ge(x_rms, m + 1)
                if m:
                    dve.wait_ge(x_turned, m)
                dve.tensor_scalar(xn[:, :], x[:, m % 4, :], st_xr[:, m:m + 1], None, ALU.mult).then_inc(xn_ready, 1)

            def modulated(m):
                s, t = m // 4, m % 4
                dve.wait_ge(x_turned, m + 1)
                if m >= 2:
                    dve.wait_ge(h_hi_ready, m - 1)
                    dve.wait_ge(h_ready, m - 1)
                for c in range(KD // 2):
                    src = ps[:, x_bank(s, t), c * P:(c + 1) * P]
                    i = dve.tensor_scalar(h32[:, m % 2, c, :], src, scale_col[:, s, c:c + 1], ada_col[:, 3 * s, c:c + 1],
                                          ALU.mult, ALU.add)
                i.then_inc(h32_ready, 1)

            def h_low(m):
                t = m % 4
                dve.wait_ge(h_hi_ready, m + 1)
                dve.tensor_tensor(h_lo[:, :, t * P:(t + 1) * P], h32[:, m % 2, :, :],
                                  h_hi[:, :, t * P:(t + 1) * P].bitcast(F32), ALU.subtract).then_inc(h_ready, 1)

            def add_start(v, k):
                j = v * KD + k
                acc = (ada_acc, upd)[v]
                dve.wait_ge(start_in[j], 16)
                if k == 0:
                    dve.tensor_scalar(acc[:, :], start_slot(j), cond[:, k:k + 1], None, ALU.mult)\
                        .then_inc(ada_added, 1)
                else:
                    dve.wait_ge(ada_added, j)
                    dve.scalar_tensor_tensor(acc[:, :], start_slot(j), cond[:, k:k + 1], acc[:, :],
                                             ALU.mult, ALU.add).then_inc(ada_added, 1)

            def add_ada(v, k):
                slot = k % 4
                dve.wait_ge(ada_in[slot], v * 32 + (16 * (k // 4) - 48))
                if k:
                    dve.wait_ge(ada_added, v * KD + k)
                if k == 0:
                    dve.wait_ge(ada_turned, v)
                    dve.tensor_scalar(ada_acc[:, :], ada_raw[:, slot, :], cond[:, k:k + 1], None, ALU.mult)\
                        .then_inc(ada_added, 1)
                else:
                    dve.scalar_tensor_tensor(ada_acc[:, :], ada_raw[:, slot, :], cond[:, k:k + 1], ada_acc[:, :],
                                             ALU.mult, ALU.add).then_inc(ada_added, 1)

            def sum_ada(v):
                dve.wait_ge(ada_turned, v + 1)
                dve.tensor_reduce(ada_col[:, :, :].rearrange("p v c -> p (v c)")[:, bass.ds(v * KD, KD)],
                                  ps[:, 0:2, :].rearrange("p b (c n) -> p (b c) n", n=P), AXIS.X, ALU.add)\
                    .then_inc(ada_summed, 1)

            def gate_up(g):
                n0, f0 = GU_BASE[g], KF * g

                def tile(i, q, straight, ada):
                    n = n0 + 2 * q + 2
                    if straight:
                        split_to(n + 4 * i + 1)
                    else:
                        split_block(i * 4 + n, n + 4)
                        split_block(i * 4 + (n + 1), n + 5)
                    if ada:
                        for k in range(4 * q, 4 * q + 4):
                            add_ada(i + 1, k)
                    dve.wait_ge(silu_done, i * 2 + (f0 + q + 1))
                    dve.tensor_tensor(a_buf[:, bass.ds(i * (2 * T) + q * T, T)], silu[:, q, :], ps[:, 5 + 2 * q, :],
                                      ALU.mult).then_inc(a_ready, 1)

                for q in range(2):
                    tile(0, q, True, False)
                with dve.Fori(1, 8) as i:
                    for q in range(2):
                        tile(i, q, False, g == 0)
                    if g == 0:
                        sum_ada(i + 1)
                if g == 0:
                    modulation()
                with dve.Fori(8, KF // 2) as i:
                    for q in range(2):
                        tile(i, q, False, False)
                split[0] = n0 + 2 * KF + LEAD

            def modulation():
                dve.wait_ge(ada_summed, 9)
                own.mark(dve.tensor_tensor(ada_col[:, 2:9, :], ada_col[:, 2:9, :],
                                           col_a[:, RA_B + 2 * KD:RA_B + 9 * KD].rearrange("p (v c) -> p v c", c=KD),
                                           ALU.add))
                own.settle()
                for s in range(3):
                    if s:
                        own.mark(dve.scalar_tensor_tensor(
                            scale_col[:, s, :], ada_col[:, 3 * s + 1, :], 1.0,
                            col_a[:, RA_G + s * KD:RA_G + (s + 1) * KD], ALU.add, ALU.mult))
                    dve.scalar_tensor_tensor(gate_col[:, s, :], ada_col[:, 3 * s + 2, :], 1.0 if s == 1 else 0.5,
                                             col_b[:, RB_GP + s * KD:RB_GP + (s + 1) * KD], ALU.mult, ALU.mult)\
                        .then_inc(gates_ready, 1)

            def down_chunk(d, hf, c):
                nch = DN_CHUNKS[d]
                split_to(DN_BASE[d] + hf * nch + c + LEAD)
                if c + LEAD < nch:
                    split_a(d, hf, c + LEAD, c + LEAD)
                elif hf == 0:
                    split_a(d, 1, c + LEAD - nch, c + LEAD - nch)

            def down(d):
                nch, n0 = DN_CHUNKS[d], DN_BASE[d]

                def chunk_loop(hf, first, last):
                    base = n0 + hf * nch
                    with dve.Fori(0, (last - first) // 4) as i:
                        for j in range(first, first + 4):
                            split_block(i * 4 + (base + j + LEAD), base + j + LEAD)
                            split_a(d, hf, i * 4 + (j + LEAD), j + LEAD)
                    split[0] = base + last + LEAD

                if nch > 8:
                    dve.wait_ge(a_ready, KF * (1 + d // 2))
                    for c in range(LEAD):
                        split_a(d, 0, c, c)
                    for c in range(4):
                        down_chunk(d, 0, c)
                    chunk_loop(0, 4, 20)
                    down_chunk(d, 0, 20)
                    down_chunk(d, 0, 21)
                else:
                    for c in range(2, nch):
                        down_chunk(d, 0, c)
                m = 4 * (d + 1)
                for c in range(8):
                    down_chunk(d, 1, c)
                    if c == 1:
                        update(4 * d)
                    if c == 2:
                        update(4 * d + 1)
                    if d < 2:
                        if c == 3:
                            norm(m)
                        if c == 4:
                            norm(m + 1)
                        if c == 5:
                            modulated(m)
                        if c == 6:
                            modulated(m + 1)
                            h_low(m)
                        if c == 7:
                            h_low(m + 1)
                if nch > 8:
                    chunk_loop(1, 8, 20)
                    down_chunk(d, 1, 20)
                    down_chunk(d, 1, 21)
                update(4 * d + 2)
                split_to(n0 + 2 * nch + 2)
                update(4 * d + 3)
                split_to(n0 + 2 * nch + 3)
                if d < 2:
                    norm(m + 2)
                    norm(m + 3)
                    modulated(m + 2)
                    modulated(m + 3)
                    h_low(m + 2)
                    h_low(m + 3)

            dve.wait_ge(cond_ready, 1)
            for k in range(KD):
                add_start(0, k)
                if k < KT:
                    norm(k)
            for k in range(KD):
                add_start(1, k)
                if k == 1:
                    sum_ada(0)
                if k == 5:
                    split_to(1)
            sum_ada(1)
            dve.wait_ge(ada_summed, 2)
            dve.wait_ge(cols_ready, 2)
            own.mark(dve.tensor_tensor(ada_col[:, 0:2, :], ada_col[:, 0:2, :],
                                       col_a[:, RA_B:RA_B + 2 * KD].rearrange("p (v c) -> p v c", c=KD), ALU.add))
            own.settle()
            dve.scalar_tensor_tensor(scale_col[:, 0, :], ada_col[:, 1, :], 1.0, col_a[:, RA_G:RA_G + KD],
                                     ALU.add, ALU.mult).then_inc(first_scale_ready, 1)
            dve.wait_ge(first_scale_ready, 1)
            for t in (0, 2):
                modulated(t)
                modulated(t + 1)
                h_low(t)
                h_low(t + 1)
                split_to(3)
            dve.wait_ge(pos_in, 16)
            own.mark(dve.tensor_copy(pos_f[:, :], pos_i[:, :]))
            own.settle()
            dve.wait_ge(consts_ready, 1)
            shape = [P, KT, MM + MP]
            own.mark(dve.tensor_tensor(ang[:, 0, :, :], pos_f[:, :].unsqueeze(2).broadcast_to(shape),
                                       inv_freq[:, :].unsqueeze(1).broadcast_to(shape), ALU.mult))
            own.settle()
            magic = 1.5 * 2.0 ** 23
            own.mark(dve.tensor_scalar(ang[:, 1, :, :], ang[:, 0, :, :], 1.0 / (2.0 * math.pi), None, ALU.mult))
            own.settle()
            own.mark(dve.tensor_scalar(ang[:, 2, :, :], ang[:, 1, :, :], magic, None, ALU.add))
            own.settle()
            own.mark(dve.tensor_scalar(ang[:, 3, :, :], ang[:, 2, :, :], magic, None, ALU.subtract))
            own.settle()
            turn1 = 6.28125
            turn2 = float(np.float32(math.floor((2 * math.pi - turn1) * 2 ** 21) / 2 ** 21))
            turn3 = float(np.float32(2 * math.pi - turn1 - turn2))
            a, b = 0, 1
            for part in (turn1, turn2, turn3):
                own.mark(dve.scalar_tensor_tensor(ang[:, b, :, :], ang[:, 3, :, :], -part, ang[:, a, :, :],
                                                  ALU.mult, ALU.add))
                own.settle()
                a, b = b, a
            limit = 3.1415925
            own.mark(dve.tensor_scalar(ang[:, a, :, :], ang[:, a, :, :], limit, -limit, ALU.min, ALU.max))
            own.settle()
            assert a == 1
            own.mark(dve.scalar_tensor_tensor(ang[:, 3, :, :], ang[:, 1, :, :], -1.0, ang[:, 1, :, :], ALU.mult, ALU.min))
            own.settle()
            dve.tensor_scalar(ang[:, 2, :, :], ang[:, 3, :, :], math.pi / 2, None, ALU.add).then_inc(sins_ready, 1)
            dve.wait_ge(residue_mult, 1)
            dve.wait_ge(masks_ready, 1)
            own.mark(dve.tensor_scalar(mask12[:, 1, :], ps[:, 2, 0:P], 1.0, -MASKED, ALU.subtract, ALU.mult))
            gate_up(0)
            down(0)

            def rotate(t1, t2, c, s, tmp, signal):
                own.mark(dve.tensor_tensor(tmp[0], t1, c, ALU.mult))
                own.mark(dve.tensor_tensor(tmp[1], t2, s, ALU.mult))
                own.mark(dve.tensor_tensor(tmp[2], t2, c, ALU.mult))
                own.mark(dve.tensor_tensor(tmp[3], t1, s, ALU.mult))
                own.settle()
                own.mark(dve.tensor_tensor(t1, tmp[0], tmp[1], ALU.subtract))
                dve.tensor_tensor(t2, tmp[2], tmp[3], ALU.add).then_inc(signal, 1)

            cos_m, sin_m = cos_t[:, :, 0:MM], sin_t[:, :, 0:MM]
            cos_p, sin_p = cos_t[:, :, MM:MM + MP], sin_t[:, :, MM:MM + MP]
            dve.wait_ge(trig_ready, 2)
            own.mark(dve.memset(k_rot[:, :, 0:NOPE], 0.0))
            for t in range(KT):
                dve.wait_ge(lat_rms, t + 1)
                own.mark(dve.tensor_scalar(lat[:, t, 0:QL], lat[:, t, 0:QL], st_latr[:, t, 0:1], None, ALU.mult))
                dve.tensor_scalar(lat[:, t, QL:QL + KVL], lat[:, t, QL:QL + KVL], st_latr[:, t, 1:2], None, ALU.mult)\
                    .then_inc(lat_normed, 1)
                if t % 2:
                    split_to(N_KV + t)
            dve.wait_ge(lat_copied, KT)
            t1, t2 = lat[:, :, QL + KVL:QL + KVL + MM], lat[:, :, QL + KVL + MM:LAT]
            tmp = [rot_m[:, j, 0:KT * MM].rearrange("p (t e) -> p t e", t=KT) for j in range(4)]
            dve.wait_ge(lat_squared, 2 * KT)
            own.mark(dve.tensor_tensor(tmp[0], t1, cos_m, ALU.mult))
            own.mark(dve.tensor_tensor(tmp[1], t2, sin_m, ALU.mult))
            own.mark(dve.tensor_tensor(tmp[2], t2, cos_m, ALU.mult))
            own.mark(dve.tensor_tensor(tmp[3], t1, sin_m, ALU.mult))
            own.settle()
            own.mark(dve.tensor_tensor(k_rot[:, :, NOPE:NOPE + MM], tmp[0], tmp[1], ALU.subtract))
            dve.tensor_tensor(k_rot[:, :, NOPE + MM:HE], tmp[2], tmp[3], ALU.add).then_inc(krot_turned, 1)
            gains = col_b[:, RB_CQ:RB_CQ + 3].unsqueeze(2).broadcast_to([P, 3, P])
            for t in range(KT):
                dve.wait_ge(lat_turned, t + 1)
                dve.tensor_tensor(c_t[:, :, t * P:(t + 1) * P],
                                  ps[:, 4 + t, 0:3 * P].rearrange("p (c n) -> p c n", n=P), gains, ALU.mult)\
                    .then_inc(c_t_ready, 1)
            dve.wait_ge(krot_hi, 2)
            for z in range(2):
                dve.tensor_tensor(mk_lo[NOPE:HE, z, :].rearrange("p (t n) -> p t n", t=KT),
                                  ps[NOPE:HE, 4:8, 3 * P:4 * P],
                                  mk_hi[NOPE:HE, z, :].rearrange("p (t n) -> p t n", t=KT).bitcast(F32),
                                  ALU.subtract).then_inc(krot_ready, 1)
            dve.wait_ge(c_hi_ready, 1)
            dve.wait_ge(c_t_ready, KT)
            dve.tensor_tensor(c_lo[:, :, :], c_t[:, :, :], c_hi[:, :, :].bitcast(F32), ALU.subtract)\
                .then_inc(c_ready, 1)
            for t in range(KT):
                dve.wait_ge(mv_hi_ready, t + 1)
                dve.tensor_tensor(mv_lo[:, t, :], ps[:, 4 + t, :], mv_hi[:, t, :].bitcast(F32), ALU.subtract)\
                    .then_inc(mv_ready, 1)
            dve.wait_ge(q_copied, KT)
            qv = q_nat[:, :, :].rearrange("p t (h e) -> p t h e", e=HE)
            wide = [P, KT, HM, MM]
            dve.wait_ge(krot_turned, 1)
            rotate(qv[:, :, :, NOPE:NOPE + MM], qv[:, :, :, NOPE + MM:HE],
                   cos_m.unsqueeze(2).broadcast_to(wide), sin_m.unsqueeze(2).broadcast_to(wide),
                   [rot_m[:, j, :].rearrange("p (t h e) -> p t h e", t=KT, h=HM) for j in range(4)], q_rotated)
            split_to(N_D0 + 3)

            def m_operands(h):
                z = h % 2
                dve.wait_ge(m_qk_hi, 2 * h + 2)
                dve.scalar_tensor_tensor(mq_lo[0:HE, z, :], ps[0:HE, 0, :], MLA_SCALE, mq_hi[0:HE, z, :].bitcast(F32),
                                         ALU.mult, ALU.subtract).then_inc(m_qk_ready, 1)
                dve.tensor_tensor(mk_lo[0:NOPE, z, :], ps[0:NOPE, 1, :], mk_hi[0:NOPE, z, :].bitcast(F32),
                                  ALU.subtract).then_inc(m_qk_ready, 1)

            m_operands(0)
            for u in range(MU + 4):
                if u < MU:
                    dve.wait_ge(m_scores, u + 1)
                    dve.tensor_reduce(mla_nm[:, u:u + 1], ps[:, 2 + u % 3, :], AXIS.X, ALU.max, negate=True)\
                        .then_inc(m_max, 1)
                v = u - 1
                if 0 <= v < MU:
                    dve.wait_ge(m_exp, v + 1)
                    own.mark(dve.reciprocal(mla_z[:, v:v + 1], mla_z[:, v:v + 1]))
                    own.settle()
                    dve.tensor_scalar(mp[:, v % 3, :], mp[:, v % 3, :], mla_z[:, v:v + 1], None, ALU.mult)\
                        .then_inc(m_normed, 1)
                v = u - 3
                if 0 <= v < MU:
                    dve.wait_ge(m_pt_hi, v + 1)
                    dst = (slice(None), v // 2 % 2, slice(None), slice(v % 2 * P, v % 2 * P + P))
                    dve.tensor_tensor(mpt_lo[dst], ps[:, 5 + v % 2, :].rearrange("p (c n) -> p c n", c=KT),
                                      mpt_hi[dst].bitcast(F32), ALU.subtract).then_inc(m_pt_ready, 1)
                if u % KT == 1 and u // KT + 1 < HM:
                    m_operands(u // KT + 1)

            split_to(N_D0 + 10)
            for t in range(KT):
                dve.wait_ge(v0_hi_ready, t + 1)
                dve.tensor_tensor(v0_lo[:, t, :], ps[:, 2 * t + 1, 0:GW], v0_hi[:, t, :].bitcast(F32), ALU.subtract)\
                    .then_inc(v0_ready, 1)

            def rotate_dilated(view, t0, nt, heads, signal):
                sh = [P, nt, heads, MP]
                tmp = [rot_d[:, j, 0:nt * heads * MP].rearrange("p (t h e) -> p t h e", t=nt, h=heads)
                       for j in range(4)]
                c = cos_p[:, t0:t0 + nt, :].unsqueeze(2).broadcast_to(sh)
                s = sin_p[:, t0:t0 + nt, :].unsqueeze(2).broadcast_to(sh)
                rotate(view[:, :, :, 0:MP], view[:, :, :, MP:2 * MP], c, s, tmp, signal)

            dve.wait_ge(d0_copied, KT)
            for t in (0, 2):
                if t:
                    dve.wait_ge(d0_rotated, 1)
                rotate_dilated(qk0[:, t:t + 2, :].rearrange("p t (h e) -> p t h e", e=E), t, 2, 2 * HG, d0_rotated)
            split_to(N_V12 + 2)
            split_to(N_V12 + 3)

            def d_operands(i):
                kind, g, _, bank, _ = PREP[i]
                parts = [(dq_lo[:, g, :], ps[:, bank, :], dq_hi[:, g, :], True)]
                parts += [(kz_lo[a * E:a * E + E, g, a, :], ps[a * E:a * E + E, bank + 1, :],
                           kz_hi[a * E:a * E + E, g, a, :], False) for a in range(2)]
                dve.wait_ge(d_qk_hi, 3 * (i + 1))
                for dst, src, hi, scaled in parts:
                    if kind == "strided":
                        dst, hi = (y.rearrange("p (r l) -> p r l", r=DIL) for y in (dst, hi))
                        src = src.rearrange("p (l r) -> p r l", r=DIL)
                    if scaled:
                        dve.scalar_tensor_tensor(dst, src, DIL_SCALE, hi.bitcast(F32), ALU.mult, ALU.subtract)\
                            .then_inc(d_qk_ready, 1)
                    else:
                        dve.tensor_tensor(dst, src, hi.bitcast(F32), ALU.subtract).then_inc(d_qk_ready, 1)

            def d_max_unit(v):
                kind, p, a, t = D_UNITS[v]
                s = v % 3
                dve.wait_ge(d_scores, v + 1)
                if v >= 3:
                    dve.wait_ge(d_pt_done, v - 2)
                if kind == "local":
                    c = chunks(t)
                    w = len(c) * P
                    rel = c[0] - t + 1
                    own.mark(dve.tensor_tensor(dp[:, s, 0:w], ps[:, 2 + s, 0:w],
                                               mask0[:, rel:rel + len(c), :].rearrange("p c n -> p (c n)"), ALU.add))
                    own.settle()
                    dve.tensor_reduce(dil_nm[:, 0, p, t, a:a + 1], dp[:, s, 0:w], AXIS.X, ALU.max, negate=True)\
                        .then_inc(d_max, 1)
                else:
                    view = "p (g a n) -> p g a n"
                    own.mark(dve.tensor_tensor(dp[:, s, :].rearrange(view, g=2, a=2),
                                               ps[:, 2 + s, :].rearrange(view, g=2, a=2),
                                               mask12[:, :, :].unsqueeze(2).broadcast_to([P, 2, 2, P]), ALU.add))
                    own.settle()
                    dve.tensor_reduce(dil_nm[:, 1, p, t, :],
                                      dp[:, s, :].rearrange("p (g a n) -> p a g n", g=2, a=2), AXIS.XY,
                                      ALU.max, negate=True).then_inc(d_max, 1)

            def d_pt_low(v):
                dve.wait_ge(d_pt_hi, v + 1)
                dve.tensor_tensor(pt_view(dpt_lo, v), pt_bank(v), pt_view(dpt_hi, v).bitcast(F32), ALU.subtract)\
                    .then_inc(d_pt_ready, 1)

            dve.wait_ge(kz_clear, 4)
            d_operands(0)
            v12n = qk12[:, :, :, :].rearrange("p t m (h e) -> p t (m h) e", e=E)
            for v in range(N_LOCAL + 4):
                if v == 2:
                    d_operands(1)
                if v < N_LOCAL:
                    d_max_unit(v)
                if 0 <= v - 3 < N_LOCAL:
                    d_pt_low(v - 3)
                if v in (4, 8, 10, 12):
                    t = (4, 8, 10, 12).index(v)
                    if t == 0:
                        dve.wait_ge(d12_copied, KT)
                        dve.wait_ge(d0_rotated, 2)
                    else:
                        dve.wait_ge(d12_rotated, t)
                    rotate_dilated(v12n[:, t:t + 1, :, :], t, 1, 4 * HG, d12_rotated)
            d_operands(2)
            d_operands(3)
            split_to(N_MRG + 2)
            for t in range(KT):
                dve.wait_ge(v12_hi_ready, t + 1)
                dve.tensor_tensor(v12_lo[:, t, :], ps[:, t, :], v12_hi[:, t, :].bitcast(F32), ALU.subtract)\
                    .then_inc(v12_ready, 1)
            split_to(N_MRG + 3)
            for v in range(N_LOCAL, len(D_UNITS) + 4):
                if v == 20:
                    d_operands(4)
                    d_operands(5)
                if v < len(D_UNITS):
                    d_max_unit(v)
                if N_LOCAL <= v - 3 < len(D_UNITS):
                    d_pt_low(v - 3)

            dve.wait_ge(d_exp, N_LOCAL + 2 * (len(D_UNITS) - N_LOCAL))
            dve.wait_ge(pv12_used, 2 * KT)
            for p, buf in enumerate((sg_a, sg_b)):
                for j, stat_ in enumerate((dil_nm, dil_z)):
                    flat = buf[:, 2 * j:2 * j + 2, :]
                    for s in range(2):
                        dve.tensor_copy(flat[:, s, :].rearrange("p (t a e) -> p t a e", t=KT, a=2, e=E),
                                        stat_[:, s, p, :, :].unsqueeze(3).broadcast_to([P, KT, 2, E]))\
                            .then_inc(mix_wide, 1)

            def mix_scales(p):
                dve.wait_ge(mix_copied, 4 * (p + 1))
                if p:
                    dve.wait_ge(mix_diff, 2 * p)
                own.mark(dve.tensor_tensor(mix_max[:, :], mix[:, p, 0, :], mix[:, p, 2, :], ALU.min))
                own.settle()
                dve.tensor_tensor(mix[:, p, 0, :], mix_max[:, :], mix[:, p, 0, :], ALU.subtract).then_inc(mix_diff, 1)
                dve.tensor_tensor(mix[:, p, 2, :], mix_max[:, :], mix[:, p, 2, :], ALU.subtract).then_inc(mix_diff, 1)

            def mix_outputs(p):
                dve.wait_ge(mix_exp, 2 * (p + 1))
                dve.wait_ge(u_copied, 4 + 4 * KT)
                e0, z0, e12, z12 = (mix[:, p, j, :] for j in range(4))
                own.mark(dve.tensor_tensor(z0, z0, e0, ALU.mult))
                own.mark(dve.tensor_tensor(z12, z12, e12, ALU.mult))
                own.mark(dve.tensor_tensor(u0[:, p, :], u0[:, p, :], e0, ALU.mult))
                own.mark(dve.tensor_tensor(u12[:, p, :], u12[:, p, :], e12, ALU.mult))
                own.settle()
                own.mark(dve.tensor_tensor(z0, z0, z12, ALU.add))
                own.mark(dve.tensor_tensor(u12[:, p, :], u12[:, p, :], u0[:, p, :], ALU.add))
                own.settle()
                own.mark(dve.reciprocal(z12, z0))
                own.settle()
                dve.tensor_tensor(u12[:, p, :], u12[:, p, :], z12, ALU.mult).then_inc(mixed, 1)

            for hf in range(2):
                n = N_MRG + hf * MRG
                ga, gb, om, od = M_BANKS[hf]
                if hf == 0:
                    mix_scales(0)
                    mix_scales(1)
                    dve.wait_ge(om_hi_ready, 1)
                    dve.tensor_tensor(om_lo[:, :, :], o_mla[:, :, :], om_hi[:, :, :].bitcast(F32), ALU.subtract)\
                        .then_inc(om_ready, 1)
                split_to(n + 7)
                if hf == 0:
                    mix_outputs(0)
                    mix_outputs(1)
                split_to(n + 10)
                split_to(n + 13)
                if hf == 0:
                    dve.wait_ge(od_hi_ready, 1)
                    dve.wait_ge(mixed, 2)
                    dve.tensor_tensor(od_lo[:, :, :], u12[:, :, :], od_hi[:, :, :].bitcast(F32), ALU.subtract)\
                        .then_inc(od_ready, 1)
                dve.wait_ge(w_used, n + 10)
                dve.wait_ge(ga_ready, KT * (hf + 1))
                for t in range(KT):
                    dve.tensor_tensor(sg_a[:, t, :], sg_a[:, t, :], ps[:, om + t, :], ALU.mult).then_inc(om_added, 1)
                split_to(n + 14)
                if hf:
                    for c in range(LEAD):
                        split_a(1, 0, c, c)
                    down_chunk(1, 0, 0)
                    down_chunk(1, 0, 1)
                dve.wait_ge(w_used, n + 11)
                dve.wait_ge(gb_ready, KT * (hf + 1))
                for t in range(KT):
                    own.mark(dve.tensor_tensor(sg_b[:, t, :], sg_b[:, t, :], ps[:, od + t, :], ALU.mult))
                own.settle()
                dve.wait_ge(om_added, KT * (hf + 1))
                for t in range(KT):
                    dve.tensor_tensor(sg_a[:, t, :], sg_a[:, t, :], sg_b[:, t, :], ALU.add).then_inc(merged, 1)
            down(1)
            gate_up(1)
            down(2)

        @block.tensor
        def _(pe):
            def product(dst, a, b, start, stop, **kw):
                (a_h, a_l), (b_h, b_l) = a, b
                pe.matmul(dst, a_h, b_h, start=start, stop=False, **kw)
                pe.matmul(dst, a_h, b_l, start=False, stop=False, **kw)
                return pe.matmul(dst, a_l, b_h, start=False, stop=stop, **kw)

            def turn(dst, src):
                n = src.shape[0]
                return pe.transpose(dst, src, ident[0:n, 0:n])

            def w(n, a, b):
                return w_hi[:, n % RING, a:b], w_lo[:, n % RING, a:b]

            def h(k, tokens):
                return h_hi[:, k, tokens], h_lo[:, k, tokens]

            def arrived(n):
                pe.wait_ge(lo_ready, n + 1)

            def turn_x(m):
                s, t = m // 4, m % 4
                pe.wait_ge(xn_ready, m + 1)
                b = x_bank(s, t)
                for c in range(KD):
                    i = turn(ps[:, b + c // 4, c % 4 * P:(c % 4 + 1) * P], xn[:, c * P:(c + 1) * P])
                i.then_inc(x_turned, 1)

            def turn_ada(v, acc=ada_acc):
                pe.wait_ge(ada_added, v * KD + KD)
                for c in range(KD):
                    i = turn(ps[:, c // 4, c % 4 * P:(c % 4 + 1) * P], acc[:, c * P:(c + 1) * P])
                i.then_inc(ada_turned, 1)

            def spread_gain(s):
                pe.wait_ge(gates_ready, 3)
                for c in range(KD):
                    i = pe.matmul(ps[:, G_BANK[s] + c // 4, c % 4 * P:(c % 4 + 1) * P],
                                  gate_col[:, s, c:c + 1].broadcast_to([P, P]), ident[:, :], start=True, stop=True)
                i.then_inc(g_spread, 1)

            def gate_up(g):
                n0, f0 = GU_BASE[g], KF * g

                def block_product(s_n, bank, tokens):
                    for k in range(KD):
                        i = product(ps[:, bank, tokens], w(s_n, k * P, (k + 1) * P), h(k, tokens), k == 0, k == KD - 1)
                    return i

                for half in range(2):
                    if half and g == 0:
                        pe.wait_ge(residue_ready, 1)
                        pe.wait_ge(h_ready, 3)
                        pe.matmul(ps[:, 2, 0:P], residue[0:DIL, :], residue[0:DIL, :], start=True, stop=True)\
                            .then_inc(residue_mult, 1)
                    if half and g:
                        turn_x(10)
                        turn_x(11)
                    pe.wait_ge(h_ready, 8 * g + 2 * half + 2)
                    tokens = slice(half * 256, half * 256 + 256)
                    for b in range(4):
                        if half == 0:
                            arrived(n0 + b)
                        i = block_product(n0 + b, 4 + b, tokens)
                        if half:
                            i.then_inc(w_used, 1)

                def tile(i, q, ada):
                    pe.wait_ge(a_ready, i * 2 + (f0 + q - 1))
                    for b in range(2):
                        s_n = n0 + 2 * q + b
                        arrived(i * 4 + s_n)
                        block_product(s_n, 4 + 2 * q + b, slice(0, T)).then_inc(w_used, 1)

                with pe.Fori(1, 8) as i:
                    for q in range(2):
                        tile(i, q, False)
                    if g == 0:
                        pe.wait_ge(ada_summed, i + 1)
                        turn_ada(i + 1)
                spread_gain(2 * g)
                with pe.Fori(8, KF // 2) as i:
                    for q in range(2):
                        tile(i, q, False)

            def down(d):
                nch, n0 = DN_CHUNKS[d], DN_BASE[d]

                def chunk(hf, c, s_c):
                    s_n = n0 + hf * nch + s_c
                    arrived(c + (n0 + hf * nch))
                    pe.wait_ge(a_lo_ready, c + (DN_COUNT[d] + hf * nch + 1))
                    slot = (hf * nch + s_c) % RING
                    for t in range(2):
                        a = tuple(y[:, slot, t * P:(t + 1) * P] for y in (a_hi, a_lo))
                        for b in range(2):
                            i = product(ps[:, y_bank(d, 2 * hf + t) + b, :], a, w(s_n, b * 512, (b + 1) * 512),
                                        s_c == 0, s_c == nch - 1)
                    i.then_inc(w_used, 1)

                def last_chunks(c0):
                    for t in range(2):
                        for c in (c0, c0 + 1):
                            arrived(n0 + nch + c)
                            pe.wait_ge(a_lo_ready, DN_COUNT[d] + nch + c + 1)
                            slot = (nch + c) % RING
                            a = tuple(y[:, slot, t * P:(t + 1) * P] for y in (a_hi, a_lo))
                            for b in range(2):
                                i = product(ps[:, y_bank(d, 2 + t) + b, :], a,
                                            w(n0 + nch + c, b * 512, (b + 1) * 512), False, c == nch - 1)
                            if t:
                                i.then_inc(w_used, 1)
                        if t == 0:
                            i.then_inc(third_summed, 1)

                def chunk_loop(hf, first, last):
                    with pe.Fori(0, (last - first) // 4) as i:
                        for j in range(first, first + 4):
                            chunk(hf, i * 4 + j, j)

                if d != 1:
                    pe.wait_ge(g_ready, d + 1)
                if nch > 8:
                    for c in range(4):
                        chunk(0, c, c)
                    chunk_loop(0, 4, 20)
                    for c in range(20, nch):
                        chunk(0, c, c)
                else:
                    pe.wait_ge(om_added, 2 * KT)
                    for c in range(4):
                        chunk(0, c, c)
                    turn_merged(1)
                    chunk(0, 4, 4)
                    pe.wait_ge(m_t_ready, KD)
                    spread_gain(1)
                    for c in range(5, nch):
                        chunk(0, c, c)
                for c in range(min(8, nch - 2)):
                    if c == 0 and d == 1:
                        pe.wait_ge(g_ready, 2)
                    if c == 0 and d != 1:
                        pe.wait_ge(a_ready, KF * (1 + d // 2))
                    chunk(1, c, c)
                    if d < 2 and c in (4, 5):
                        turn_x(4 * (d + 1) + c - 4)
                if nch > 8:
                    chunk_loop(1, 8, 20)
                last_chunks(nch - 2)

            pe.wait_ge(consts_ready, 1)
            pe.wait_ge(rows_a_in, 16 * 5)
            turn(ps[:, 0, 0:RA_N], rows_a[0:RA_N, :]).then_inc(rows_turned, 1)
            turn_x(0)
            turn_x(1)
            pe.wait_ge(rows_b_in, 16 * 5)
            turn(ps[:, 1, 0:RB_N], rows_b[0:RB_N, :]).then_inc(rows_turned, 1)
            turn_x(2)
            pe.wait_ge(cols_ready, 2)
            turn_ada(0)
            pe.wait_ge(ada_summed, 1)
            turn_ada(1, upd)
            pe.wait_ge(ada_summed, 2)
            turn_x(3)
            gate_up(0)
            down(0)

            for half in range(2):
                if half:
                    turn_x(6)
                    turn_x(7)
                pe.wait_ge(h_ready, 4 + 2 * half + 2)
                for b in range(KD // 2):
                    n = N_LAT + b
                    if half == 0:
                        arrived(n)
                    for kk in range(2):
                        k = 2 * b + kk
                        for t in (2 * half, 2 * half + 1):
                            i = product(ps[:, t, 0:LAT], h(k, slice(t * P, (t + 1) * P)),
                                        w(n, kk * LAT, (kk + 1) * LAT), k == 0, k == KD - 1)
                    if half:
                        i.then_inc(w_used, 1)
                if half == 0:
                    i.then_inc(lat_half, 1)
            for t in range(KT):
                pe.wait_ge(lat_normed, t + 1)
                for c in range(3):
                    turn(ps[:, 4 + t, c * P:(c + 1) * P], lat[:, t, c * P:(c + 1) * P])
                if t == 0:
                    pe.wait_ge(krot_turned, 1)
                turn(ps[0:HE, 4 + t, 3 * P:4 * P], k_rot[:, t, :]).then_inc(lat_turned, 1)
            arrived(N_KV)
            pe.wait_ge(c_ready, 1)
            pe.wait_ge(krot_ready, 2)
            ukv = [y[:, :].rearrange("p (h e) -> p h e", e=P) for y in (ukv_hi, ukv_lo)]
            for t in range(KT):
                i = product(ps[:, 4 + t, :].rearrange("p (h e) -> p h e", e=VD),
                            tuple(y[:, 2, t * P:(t + 1) * P] for y in (c_hi, c_lo)),
                            tuple(y[:, :, NOPE:P] for y in ukv), True, True)
                i.then_inc(mv_done if t < KT - 1 else w_used, 1)
            arrived(N_UQ + 1)
            for t in range(KT):
                if t == 2:
                    pe.wait_ge(mv_ready, KT)
                for k in range(2):
                    for b in range(2):
                        i = product(ps[:, 2 * t + b, 0:384], tuple(y[:, k, t * P:(t + 1) * P] for y in (c_hi, c_lo)),
                                    w(N_UQ + k, b * 384, (b + 1) * 384), k == 0, k == 1)
                    if t == KT - 1:
                        i.then_inc(w_used, 1)
                if t < KT - 1:
                    i.then_inc(uq_done, 1)

            def m_operands(hd):
                if hd == 0:
                    pe.wait_ge(q_rotated, 1)
                else:
                    pe.wait_ge(m_qk_ready, 2 * hd)
                for t in range(KT):
                    turn(ps[0:HE, 0, t * P:(t + 1) * P], q_nat[:, t, hd * HE:(hd + 1) * HE])
                product(ps[:, 1, :], tuple(y[:, hd * P:(hd + 1) * P] for y in (ukv_hi, ukv_lo)),
                        tuple(y[:, 2, :] for y in (c_hi, c_lo)), True, True).then_inc(m_turned, 1)

            def m_values(j):
                hd, half = j // 2, j % 2
                pe.wait_ge(m_pt_ready, 2 * j + 2)
                if half == 0 and hd:
                    pe.wait_ge(m_out_copied, hd)
                for c in range(KT):
                    i = product(ps[:, 7, half * 256:half * 256 + 256],
                                tuple(y[:, c, hd // 2 * P:(hd // 2 + 1) * P] for y in (mv_hi, mv_lo)),
                                tuple(y[:, j % 2, c, :] for y in (mpt_hi, mpt_lo)), c == 0, c == KT - 1)
                i.then_inc(m_pv, 1)

            m_operands(0)
            for u in range(MU + 4):
                if u % KT == 1 and u // KT + 1 < HM:
                    m_operands(u // KT + 1)
                if u < MU:
                    hd, t = u // KT, u % KT
                    pe.wait_ge(m_qk_ready, 2 * hd + 2)
                    if u >= 3:
                        pe.wait_ge(m_exp, u - 2)
                    product(ps[:, 2 + u % 3, :], tuple(y[0:HE, hd % 2, t * P:(t + 1) * P] for y in (mq_hi, mq_lo)),
                            tuple(y[0:HE, hd % 2, :] for y in (mk_hi, mk_lo)), True, True).then_inc(m_scores, 1)
                v = u - 3
                if 0 <= v < MU:
                    pe.wait_ge(m_normed, v + 1)
                    if v >= 2:
                        pe.wait_ge(m_pt_ready, v - 1)
                    for c in range(KT):
                        i = turn(ps[:, 5 + v % 2, c * P:(c + 1) * P], mp[:, v % 3, c * P:(c + 1) * P])
                    i.then_inc(m_pt_done, 1)
                v = u - 4
                if v >= 0 and v % 2:
                    m_values(v // 2)

            for k in range(KD):
                n = N_D0 + k
                arrived(n)
                if k == 0:
                    pe.wait_ge(m_out_copied, HM)
                for t in range(KT):
                    for b, (lo, hi) in enumerate(((0, 2 * GW), (2 * GW, 3 * GW))):
                        i = product(ps[:, 2 * t + b, 0:hi - lo], h(k, slice(t * P, (t + 1) * P)), w(n, lo, hi),
                                    k == 0, k == KD - 1)
                i.then_inc(w_used, 1)
            for k in range(KD):
                n = N_D12 + k
                arrived(n)
                for t in range(KT):
                    if k == 0:
                        pe.wait_ge(d0_copied, t + 1)
                        pe.wait_ge(v0_ready, t + 1)
                    for b in range(2):
                        i = product(ps[:, 2 * t + b, :], h(k, slice(t * P, (t + 1) * P)), w(n, b * 512, (b + 1) * 512),
                                    k == 0, k == KD - 1)
                i.then_inc(w_used, 1)

            def d_operands(i):
                kind, g, p, bank, _ = PREP[i]
                if kind == "local":
                    pe.wait_ge(d0_rotated, 2)
                else:
                    pe.wait_ge(d12_rotated, KT)
                if i in (1, 4, 5):
                    pe.wait_ge(d_qk_ready, 3 * i)
                for m in range(2):
                    for t in range(KT):
                        if kind == "local":
                            src = qk0[:, t, m * GW + p * P:m * GW + (p + 1) * P]
                        else:
                            src = qk12[:, t, m, g * GW + p * P:g * GW + (p + 1) * P]
                        j = turn(ps[:, bank + m, t * P:(t + 1) * P], src)
                j.then_inc(d_turned, 1)

            def d_scores_unit(v):
                kind, p, a, t = D_UNITS[v]
                if v >= 3:
                    pe.wait_ge(d_max, v - 2)
                bank = 2 + v % 3
                if kind == "local":
                    pe.wait_ge(d_qk_ready, 3 * (p + 1))
                    c = chunks(t)
                    cols = slice(c[0] * P, (c[-1] + 1) * P)
                    product(ps[:, bank, 0:len(c) * P], tuple(y[:, p, t * P:(t + 1) * P] for y in (dq_hi, dq_lo)),
                            tuple(y[:, p, a, cols] for y in (kz_hi, kz_lo)), True, True).then_inc(d_scores, 1)
                    return
                for g in range(2):
                    pe.wait_ge(d_qk_ready, 3 * (2 * p + g + 3))
                    i = product(ps[:, bank, g * 256:(g + 1) * 256].rearrange("p (a n) -> p a n", a=2),
                                tuple(y[:, g, t * P:(t + 1) * P] for y in (dq_hi, dq_lo)),
                                tuple(y[:, g, :, t * P:(t + 1) * P] for y in (kz_hi, kz_lo)), True, True)
                i.then_inc(d_scores, 1)

            def d_turn_unit(v):
                kind, _, _, t = D_UNITS[v]
                n = len(chunks(t)) if kind == "local" else 4
                pe.wait_ge(d_exp, v + 1 if v < N_LOCAL else N_LOCAL + 2 * (v - N_LOCAL + 1))
                if v >= 2:
                    pe.wait_ge(d_pt_ready, v - 1)
                for c in range(n):
                    i = turn(ps[:, 5 + v % 2, c * P:(c + 1) * P], dp[:, v % 3, c * P:(c + 1) * P])
                i.then_inc(d_pt_done, 1)

            def d_values(v):
                kind, p, a, t = D_UNITS[v]
                pe.wait_ge(d_pt_ready, v + 1)
                if kind == "local":
                    for kc in pv0_steps(t):
                        q = chunks(kc)
                        cols = slice(q[0] * P, (q[-1] + 1) * P)
                        if kc == 0 and v >= KT:
                            pe.wait_ge(u_copied, v // KT)
                        product(ps[:, 7, cols], tuple(y[:, kc, p * P:(p + 1) * P] for y in (v0_hi, v0_lo)),
                                tuple(y[:, kc, cols] for y in (dpt_hi, dpt_lo)), kc == 0, kc == KT - 1,
                                skip_group_check=True).then_inc(pv0_used, 1)
                    return
                wv = v - N_LOCAL
                pe.wait_ge(u_copied, 4 + 2 * wv)
                for g in range(2):
                    i = product(ps[:, 7, t % 2 * 256:(t % 2 + 1) * 256],
                                tuple(y[:, t, g * GW + p * P:g * GW + (p + 1) * P] for y in (v12_hi, v12_lo)),
                                tuple(y[:, wv % KT, g * 256:(g + 1) * 256] for y in (dpt_hi, dpt_lo)),
                                g == 0, g == 1)
                i.then_inc(pv12_used, 1)

            pe.wait_ge(d12_copied, KT)
            d_operands(0)
            for v in range(N_LOCAL + 4):
                if v == 2:
                    d_operands(1)
                if v < N_LOCAL:
                    d_scores_unit(v)
                if 0 <= v - 3 < N_LOCAL:
                    d_turn_unit(v - 3)
                if v - 4 >= 0:
                    d_values(v - 4)
            pe.wait_ge(u_copied, 4)
            pe.wait_ge(d_pt_ready, N_LOCAL)
            d_operands(2)
            d_operands(3)
            for b in range(KD // 2):
                n = N_V12 + b
                arrived(n)
                for kk in range(2):
                    k = 2 * b + kk
                    for r in range(KT):
                        i = product(ps[:, r, :], h(k, slice(r, T, DIL)), w(n, kk * 512, (kk + 1) * 512),
                                    k == 0, k == KD - 1)
                i.then_inc(w_used, 1)
            pe.wait_ge(v12_ready, KT)
            for v in range(N_LOCAL, len(D_UNITS) + 4):
                if v == 20:
                    d_operands(4)
                    d_operands(5)
                if v < len(D_UNITS):
                    d_scores_unit(v)
                if N_LOCAL <= v - 3 < len(D_UNITS):
                    d_turn_unit(v - 3)
                if v - 4 >= N_LOCAL:
                    d_values(v - 4)

            pe.wait_ge(u_copied, 4 + 4 * KT)
            for p, buf in enumerate((sg_a, sg_b)):
                pe.wait_ge(mix_wide, 4 * (p + 1))
                for j, src in enumerate((0, 2, 1, 3)):
                    for t in range(KT):
                        i = pe.matmul(ps[:, 4 * p + j, t * P:(t + 1) * P], buf[:, src, t * P:(t + 1) * P],
                                      ident[:, :], start=True, stop=True)
                i.then_inc(mix_spread, 1)

            def turn_merged(hf):
                pe.wait_ge(merged, KT * (hf + 1))
                for c in range(4):
                    for t in range(KT):
                        i = turn(ps[:, c, t * P:(t + 1) * P], sg_a[:, t, c * P:(c + 1) * P])
                    i.then_inc(m_t_done, 1)

            for hf in range(2):
                n = N_MRG + hf * MRG
                ga, gb, om, od = M_BANKS[hf]
                for m, bank in ((0, ga), (1, gb)):
                    if hf == 0:
                        pe.wait_ge(mix_copied, 4 * (m + 1))
                    elif m == 0:
                        pe.wait_ge(merged, 1)
                    else:
                        pe.wait_ge(m_t_ready, 4)
                    for b in range(KD // 2):
                        if hf and m == 0 and b == 2:
                            turn_merged(0)
                        arrived(n + 4 * m + b)
                        for kk in range(2):
                            k = 2 * b + kk
                            for t in range(KT):
                                i = product(ps[:, bank + t, :], h(k, slice(t * P, (t + 1) * P)),
                                            w(n + 4 * m + b, kk * 512, (kk + 1) * 512), k == 0, k == KD - 1)
                        i.then_inc(w_used, 1)
                pe.wait_ge(ga_ready, KT * (hf + 1))
                pe.wait_ge(om_ready, 1)
                for b in range(2):
                    arrived(n + 8 + b)
                    for kk in range(2):
                        c = 2 * b + kk
                        for t in range(KT):
                            i = product(ps[:, om + t, :], tuple(y[:, c, t * P:(t + 1) * P] for y in (om_hi, om_lo)),
                                        w(n + 8 + b, kk * 512, (kk + 1) * 512), c == 0, c == 3)
                    i.then_inc(w_used, 1)
                pe.wait_ge(gb_ready, KT * (hf + 1))
                pe.wait_ge(od_ready, 1)
                arrived(n + 10)
                for c in range(2):
                    for t in range(KT):
                        i = product(ps[:, od + t, :], tuple(y[:, c, t * P:(t + 1) * P] for y in (od_hi, od_lo)),
                                    w(n + 10, c * 512, (c + 1) * 512), c == 0, c == 1)
                i.then_inc(w_used, 1)
            down(1)
            gate_up(1)
            down(2)


def kernel(**inputs):
    import concourse.bacc as bacc
    from concourse.bass_utils import run_bass_kernel_spmd

    nc = bacc.Bacc("TRN2", target_bir_lowering=False, num_devices=1)
    arrays, args = {}, {}
    for name in inputs:
        a = np.ascontiguousarray(inputs[name])
        arrays[f"in_{name}"] = a
        args[name] = nc.dram_tensor(f"in_{name}", a.shape, mybir.dt.from_np(a.dtype), kind="ExternalInput").ap()
    shape = inputs["x"].shape
    out = nc.dram_tensor("out", shape, F32, kind="ExternalOutput").ap()
    encoder_block(nc, args, out)
    r = run_bass_kernel_spmd(nc, [arrays], core_ids=[0])
    return r.results[0]["out"]
```

```python
import math
from contextlib import ExitStack

import numpy as np

import concourse.bass as bass
from concourse import mybir

F32 = mybir.dt.float32
F32R = mybir.dt.float32r
I32 = mybir.dt.int32
ALU = mybir.AluOpType
ACT = mybir.ActivationFunctionType
AXIS = mybir.AxisListType

P = 128
EPS = 1e-6
MASKED = -1e30


class Steps:

    def __init__(self, engine, sem):
        self.engine, self.sem, self.n = engine, sem, 0

    def mark(self, instruction):
        self.n += 1
        return instruction.then_inc(self.sem, 1)

    def settle(self):
        self.engine.wait_ge(self.sem, self.n)


def encoder_block(nc, ins, out):
    D = ins["x"].shape[2]
    T = ins["x"].shape[1]
    FF = ins["w_gate1"].shape[2]
    KD, KT, KF = D // P, T // P, FF // P
    QL = ins["g_cq"].shape[1]
    KVL = ins["g_ckv"].shape[1]
    NOPE, ROPE, VD = 64, 32, 64
    HM = ins["w_uq"].shape[2] // (NOPE + ROPE)
    HE = NOPE + ROPE
    MLA_SCALE = float(HE) ** -0.5
    G, HG, E = 3, 4, 64
    GW = HG * E
    DIL_SCALE = float(E) ** -0.5
    RP = E // 4
    OFF_DIL = QL + KVL + ROPE
    OFF_GATE = OFF_DIL + 3 * G * GW
    LAT = OFF_DIL
    MM, MP = ROPE // 2, RP // 2
    DIL = 4
    assert (D, T, FF) == (1024, 512, 2816)

    N_GU1 = 0
    N_DN1 = N_GU1 + 2 * KF
    N_LAT = N_DN1 + 2 * KF
    N_KV = N_LAT + KD // 2
    N_UQ = N_KV + 1
    N_D0 = N_UQ + QL // P
    N_D12 = N_D0 + KD
    N_V12 = N_D12 + KD
    N_MRG = N_V12 + KD // 2
    MRG = 11
    N_OUT = N_MRG + 2 * MRG
    N_GU2 = N_OUT + 2 * KD
    N_DN2 = N_GU2 + 2 * KF
    N_END = N_DN2 + 2 * KF
    RING = 4
    LEAD = 2
    TOP_WORDS = 23032

    GU_BASE = (N_GU1, N_GU2)
    DN_BASE = (N_DN1, N_OUT, N_DN2)
    DN_CHUNKS = (KF, KD, KF)
    DN_COUNT = (0, 2 * KF, 2 * KF + 2 * KD)
    Y_BANK = ((0, 4), (4, 0), (0, 4))

    def y_bank(d, t):
        return Y_BANK[d][t // 2] + 2 * (t % 2)

    def x_bank(s, t):
        return (4, 6, 2, 0)[t] if s == 0 else y_bank(s - 1, t)

    w_gu = [[ins[n][0].rearrange("(k p) f -> p k f", p=P) for n in ("w_gate" + q, "w_up" + q)] for q in "12"]
    w_dn = [ins["w_down1"][0], ins["w_out"][0], ins["w_down2"][0]]
    w_in = ins["w_in"][0].rearrange("(k p) f -> p k f", p=P)
    w_ada = ins["w_ada"][0]

    with ExitStack() as ctx:
        def sem(name):
            return ctx.enter_context(nc.semaphore(name))

        def sb(scope, name, shape, dt=F32):
            return scope.enter_context(nc.sbuf_tensor(name, shape, dt))

        dil_nm = sb(ctx, "dil_nm", [P, 2, 2, KT, 2])
        dil_z = sb(ctx, "dil_z", [P, 2, 2, KT, 2])
        x = sb(ctx, "x_resid", [P, KT, D])
        w_raw = sb(ctx, "w_raw", [P, RING, 1024])
        w_hi = sb(ctx, "w_hi", [P, RING, 1024], F32R)
        w_lo = sb(ctx, "w_lo", [P, RING, 1024], F32R)
        h_hi = sb(ctx, "h_hi", [P, KD, T], F32R)
        h_lo = sb(ctx, "h_lo", [P, KD, T], F32R)
        ident = sb(ctx, "ident", [P, P])
        RA_B, RA_C, RA_G = 0, 9 * KD, 10 * KD
        RA_N = 13 * KD
        RB_GP, RB_CQ, RB_CKV = 0, 3 * KD, 3 * KD + QL // P
        RB_N = RB_CKV + 1
        col_a = sb(ctx, "col_a", [P, RA_N])
        col_b = sb(ctx, "col_b", [P, RB_N])
        cond = sb(ctx, "cond", [P, KD])
        ada_col = sb(ctx, "ada_col", [P, 9, KD])
        scale_col = sb(ctx, "scale_col", [P, 3, KD])
        gate_col = sb(ctx, "gate_col", [P, 3, KD])
        stat = sb(ctx, "stat", [P, 160])
        neg_half = sb(ctx, "neg_half", [P, 2])
        pos_i = sb(ctx, "pos_i", [P, KT], I32)
        pos_f = sb(ctx, "pos_f", [P, KT])
        inv_freq = sb(ctx, "inv_freq", [P, MM + MP])
        cos_t = sb(ctx, "cos_t", [P, KT, MM + MP])
        sin_t = sb(ctx, "sin_t", [P, KT, MM + MP])
        mask0 = sb(ctx, "mask0", [P, 3, P])
        mask12 = sb(ctx, "mask12", [P, 2, P])

        with ExitStack() as s:
            sb(s, "below_the_top", [P, TOP_WORDS])
            o_mla = sb(s, "o_mla", [P, HM // 2, T])
            u12 = sb(s, "u12", [P, 2, T])
            u0 = sb(s, "u0", [P, 2, T])

        with ExitStack() as s:
            q_nat = sb(s, "q_nat", [P, KT, HM * HE])
            c_hi = sb(s, "c_hi", [P, 3, T], F32R)
            c_lo = sb(s, "c_lo", [P, 3, T], F32R)
            ukv_hi = sb(s, "ukv_hi", [P, 1024], F32R)
            ukv_lo = sb(s, "ukv_lo", [P, 1024], F32R)
            mq_hi = sb(s, "mq_hi", [P, 2, T], F32R)
            mq_lo = sb(s, "mq_lo", [P, 2, T], F32R)
            mk_hi = sb(s, "mk_hi", [P, 2, T], F32R)
            mk_lo = sb(s, "mk_lo", [P, 2, T], F32R)
            mv_hi = sb(s, "mv_hi", [P, KT, HM * VD], F32R)
            mv_lo = sb(s, "mv_lo", [P, KT, HM * VD], F32R)
            with ExitStack() as s2:
                k_rot = sb(s2, "k_rot", [P, KT, HE])
                lat = sb(s2, "lat", [P, KT, LAT])
                c_t = sb(s2, "c_t", [P, 3, T])
                rot_m = sb(s2, "rot_m", [P, 4, KT * HM * MM])
            with ExitStack() as s2:
                mp = sb(s2, "mla_p", [P, 3, T])
                mpt_hi = sb(s2, "mla_pt_hi", [P, 2, KT, 256], F32R)
                mpt_lo = sb(s2, "mla_pt_lo", [P, 2, KT, 256], F32R)
        with ExitStack() as s:
            mix_cols = sb(s, "mix_cols", [P, 2, 4, T])
        with ExitStack() as s:
            qk12 = sb(s, "qk12", [P, KT, 2, 2 * GW])
            dq_hi = sb(s, "dq_hi", [P, 2, T], F32R)
            dq_lo = sb(s, "dq_lo", [P, 2, T], F32R)
            kz_hi = sb(s, "kz_hi", [P, 2, 2, T], F32R)
            kz_lo = sb(s, "kz_lo", [P, 2, 2, T], F32R)
            dpt_hi = sb(s, "dpt_hi", [P, KT, T], F32R)
            dpt_lo = sb(s, "dpt_lo", [P, KT, T], F32R)
            dp = sb(s, "dil_p", [P, 3, T])
            rot_d = sb(s, "rot_d", [P, 4, 4 * HG * MP])
            v0_hi = sb(s, "v0_hi", [P, KT, GW], F32R)
            v0_lo = sb(s, "v0_lo", [P, KT, GW], F32R)
            v12b_hi = sb(s, "v12b_hi", [P, 2, 2 * GW], F32R)
            v12b_lo = sb(s, "v12b_lo", [P, 2, 2 * GW], F32R)
            with ExitStack() as s2:
                qk0 = sb(s2, "qk0", [P, KT, 2 * GW])
            with ExitStack() as s2:
                v12a_hi = sb(s2, "v12a_hi", [P, 2, 2 * GW], F32R)
                v12a_lo = sb(s2, "v12a_lo", [P, 2, 2 * GW], F32R)
        g_row = sb(ctx, "g_row", [P, D])
        with ExitStack() as s:
            junk = sb(s, "junk", [P, D])
            upd = sb(s, "upd", [P, D])
            xn = sb(s, "xn", [P, D])
            h32 = sb(s, "h32", [P, 2, KD, P])
            a_hi = sb(s, "a_hi", [P, RING, 256], F32R)
            a_lo = sb(s, "a_lo", [P, RING, 256], F32R)
            with ExitStack() as s2:
                a_buf = sb(s2, "a_buf", [P, KF * T])
                silu = sb(s2, "silu", [P, 2, T])
                ada_raw = sb(s2, "ada_raw", [P, 4, D])
                ada_acc = sb(s2, "ada_acc", [P, D])
                rows_a = sb(s2, "rows_a", [P, P])
                rows_b = sb(s2, "rows_b", [P, P])
                ang = sb(s2, "ang", [P, 4, KT, MM + MP])
                residue = sb(s2, "residue", [P, P])
            with ExitStack() as s2:
                m_t = sb(s2, "m_t", [P, KD * T])
                sg_a = sb(s2, "sg_a", [P, KT, T])
                sg_b = sb(s2, "sg_b", [P, KT, T])
                mix_max = sb(s2, "mix_max", [P, T])
                mix = sb(s2, "mix", [P, 2, 4, T])
        with ExitStack() as s:
            od_hi = sb(s, "od_hi", [P, 2, T], F32R)
            od_lo = sb(s, "od_lo", [P, 2, T], F32R)
            om_hi = sb(s, "om_hi", [P, HM // 2, T], F32R)
            om_lo = sb(s, "om_lo", [P, HM // 2, T], F32R)
        ps = ctx.enter_context(nc.psum_tensor("ps", [P, 8, 512], F32))

        st_y = stat[:, 0:12]
        st_yr = stat[:, 12:24]
        st_x = stat[:, 24:40]
        st_xr = stat[:, 40:56]
        st_eps = stat[:, 56:64]
        st_lat = stat[:, 64:72].rearrange("p (t c) -> p t c", c=2)
        st_latr = stat[:, 72:80].rearrange("p (t c) -> p t c", c=2)
        mla_nm = stat[:, 80:112]
        mla_z = stat[:, 112:144]

        x_in = [sem(f"x_in{t}") for t in range(KT)]
        rows_a_in = sem("rows_a_in")
        rows_b_in = sem("rows_b_in")
        pos_in = sem("pos_in")
        raw_in = [sem(f"raw_in{i}") for i in range(RING)]
        hi_ready = sem("hi_ready")
        lo_ready = sem("lo_ready")
        w_used = sem("w_used")
        start_in = [sem(f"start_in{i}") for i in range(2 * KD)]
        ada_in = [sem(f"ada_in{i}") for i in range(4)]
        ada_added = sem("ada_added")
        ada_turned = sem("ada_turned")
        ada_summed = sem("ada_summed")
        consts_ready = sem("consts_ready")
        masks_ready = sem("masks_ready")
        residue_ready = sem("residue_ready")
        rows_turned = sem("rows_turned")
        cols_ready = sem("cols_ready")
        cond_ready = sem("cond_ready")
        gates_ready = sem("gates_ready")
        sins_ready = sem("sins_ready")
        trig_ready = sem("trig_ready")
        g_spread = sem("g_spread")
        g_ready = sem("g_ready")
        silu_done = sem("silu_done")
        a_ready = sem("a_ready")
        a_hi_ready = sem("a_hi_ready")
        a_lo_ready = sem("a_lo_ready")
        y_squared = sem("y_squared")
        y_rms = sem("y_rms")
        x_new = sem("x_new")
        x_squared = sem("x_squared")
        x_rms = sem("x_rms")
        xn_ready = sem("xn_ready")
        third_summed = sem("third_summed")
        v12_half = sem("v12_half")
        x_turned = sem("x_turned")
        h32_ready = sem("h32_ready")
        h32_upper_ready = sem("h32_upper_ready")
        first_scale_ready = sem("first_scale_ready")
        h_hi_ready = sem("h_hi_ready")
        h_ready = sem("h_ready")
        lat_copied = sem("lat_copied")
        lat_squared = sem("lat_squared")
        lat_rms = sem("lat_rms")
        lat_normed = sem("lat_normed")
        lat_turned = sem("lat_turned")
        c_t_ready = sem("c_t_ready")
        c_hi_ready = sem("c_hi_ready")
        c_ready = sem("c_ready")
        krot_hi = sem("krot_hi")
        krot_turned = sem("krot_turned")
        residue_mult = sem("residue_mult")
        krot_ready = sem("krot_ready")
        mv_done = sem("mv_done")
        mv_hi_ready = sem("mv_hi_ready")
        mv_ready = sem("mv_ready")
        uq_done = sem("uq_done")
        lat_summed = sem("lat_summed")
        m_pv = sem("m_pv")
        pv12_used = sem("pv12_used")
        mix_wide = sem("mix_wide")
        q_copied = sem("q_copied")
        q_rotated = sem("q_rotated")
        m_turned = sem("m_turned")
        m_qk_hi = sem("m_qk_hi")
        m_qk_ready = sem("m_qk_ready")
        m_scores = sem("m_scores")
        m_max = sem("m_max")
        m_exp = sem("m_exp")
        m_normed = sem("m_normed")
        m_pt_done = sem("m_pt_done")
        m_pt_hi = sem("m_pt_hi")
        m_pt_ready = sem("m_pt_ready")
        m_out_copied = sem("m_out_copied")
        d0_copied = sem("d0_copied")
        v0_hi_ready = sem("v0_hi_ready")
        v0_ready = sem("v0_ready")
        d0_rotated = sem("d0_rotated")
        d12_copied = sem("d12_copied")
        d12_rotated = sem("d12_rotated")
        v12_hi_ready = sem("v12_hi_ready")
        v12_ready = sem("v12_ready")
        kz_clear = sem("kz_clear")
        d_turned = sem("d_turned")
        d_qk_hi = sem("d_qk_hi")
        d_qk_ready = sem("d_qk_ready")
        d_scores = sem("d_scores")
        d_max = sem("d_max")
        d_exp = sem("d_exp")
        d_pt_done = sem("d_pt_done")
        d_pt_hi = sem("d_pt_hi")
        d_pt_ready = sem("d_pt_ready")
        pv0_used = sem("pv0_used")
        u_copied = sem("u_copied")
        mix_spread = sem("mix_spread")
        mix_copied = sem("mix_copied")
        mix_diff = sem("mix_diff")
        mix_exp = sem("mix_exp")
        mixed = sem("mixed")
        om_hi_ready = sem("om_hi_ready")
        om_ready = sem("om_ready")
        od_hi_ready = sem("od_hi_ready")
        od_ready = sem("od_ready")
        ga_ready = sem("ga_ready")
        gb_ready = sem("gb_ready")
        om_gated = sem("om_gated")
        merged = sem("merged")
        od_gated = sem("od_gated")
        m_t_done = sem("m_t_done")
        m_t_ready = sem("m_t_ready")
        dve_own = sem("dve_own")
        pool_own = sem("pool_own")
        out_written = sem("out_written")

        MU = HM * KT
        D_UNITS = [("local", p, a, t) for p in range(2) for a in range(2) for t in range(KT)] \
            + [("strided", p, 0, r) for p in range(2) for r in range(KT)]
        N_LOCAL = 4 * KT

        def chunks(t):
            return range(max(0, t - 1), min(KT, t + 2))

        def pv0_steps(t):
            return [] if t == 0 else [t - 1] if t < KT - 1 else [t - 1, t]

        PREP = [("local", 0, 0, 0, 0), ("local", 1, 1, 5, 0), ("strided", 0, 0, 0, 8), ("strided", 1, 0, 3, 16),
                ("strided", 0, 1, 0, 20), ("strided", 1, 1, 2, 20)]
        PREP_AT = {1: (1,), 12: (2,), 16: (3,), 20: (4, 5)}
        ROTATE_AT = (3, 5, 7, 9)
        V12_COUNTS = {v: 2 for v in range(1, 9)} | {14: 4, 15: 4, 16: 5, 17: 3}
        V12_COPIES = {10: (0, 1), 18: (2, 3)}

        def v12(r):
            hi, lo = ((v12a_hi, v12a_lo), (v12b_hi, v12b_lo))[r // 2]
            return hi[:, r % 2, :], lo[:, r % 2, :]
        STAGED = KF * T // D
        UQ_BANK = (0, 6, 0, 6)
        M_BANKS = ((0, 4, 0, 4), (4, 0, 4, 0))
        G_BANK = (2, 0, 2)

        def w_shape(n):
            if N_LAT <= n < N_KV:
                return 2 * LAT
            if N_UQ <= n < N_D12:
                return 768
            return 1024

        def pt_view(buf, v):
            kind, _, _, t = D_UNITS[v]
            if kind == "local":
                c = chunks(t)
                return buf[:, c[0]:c[-1] + 1, t * P:(t + 1) * P]
            return buf[:, v % KT, :]

        def pt_bank(v):
            kind, _, _, t = D_UNITS[v]
            if kind == "local":
                return ps[:, 5 + v % 2, 0:len(chunks(t)) * P].rearrange("p (c n) -> p c n", n=P)
            return ps[:, 5 + v % 2, :]

        def pt_free(v):
            if v < N_LOCAL:
                h, t = v // KT, v % KT
                return pv0_used, max(0, KT * (h - 1) + min(t + 2, KT)) if h else 0
            return (pv0_used, v - KT + 1) if v < N_LOCAL + KT else (pv12_used, v - N_LOCAL - KT + 1)

        def start_slot(j):
            return a_buf[:, j * D:(j + 1) * D] if j < STAGED else ada_raw[:, j % 4, :]

        block = ctx.enter_context(nc.Block())

        @block.sync
        def _(sp):
            def slot_free(n):
                sp.wait_ge(lo_ready, n - RING + 1)

            def load(static_n, dst, src):
                sp.dma_start(dst, src).then_inc(raw_in[static_n % RING], 16)

            def load_tile(g, i, q, first=False):
                for m in range(2):
                    s_n = GU_BASE[g] + 2 * q + m
                    if not first:
                        slot_free(i * 4 + s_n)
                    dst = w_raw[:, s_n % RING, :].rearrange("p (k f) -> p k f", k=KD)
                    load(s_n, dst, w_gu[g][m][:, :, bass.ds(i * (2 * P) + q * P, P)])

            def load_ada(v, k):
                sp.wait_ge(ada_added, v * KD + (k - 3))
                sp.dma_start(ada_raw[:, k % 4, :], w_ada[k * P:(k + 1) * P, bass.ds(v * D, D)])\
                    .then_inc(ada_in[k % 4], 16)

            def row(dst, name, a, n, signal):
                sp.dma_start(dst[a:a + n, :], ins[name][0].rearrange("(r e) -> r e", e=P)).then_inc(signal, 16)

            def load_start(j):
                if j >= STAGED + 4:
                    sp.wait_ge(ada_added, j - 3)
                v, k = j // KD, j % KD
                sp.dma_start(start_slot(j), w_ada[k * P:(k + 1) * P, v * D:(v + 1) * D]).then_inc(start_in[j], 16)

            def load_x(t):
                sp.dma_start(x[:, t, :], ins["x"][0, t * P:(t + 1) * P, :]).then_inc(x_in[t], 16)

            row(rows_a, "c", RA_C, KD, rows_a_in)
            row(rows_a, "b_ada", RA_B, 9 * KD, rows_a_in)
            for s, name in enumerate(("g_pre_ff1", "g_pre_mix", "g_pre_ff2")):
                row(rows_a, name, RA_G + s * KD, KD, rows_a_in)
            load_start(0)
            load_x(0)
            load_start(1)
            load_x(1)
            for s, name in enumerate(("g_post_ff1", "g_post_mix", "g_post_ff2")):
                row(rows_b, name, RB_GP + s * KD, KD, rows_b_in)
            row(rows_b, "g_cq", RB_CQ, QL // P, rows_b_in)
            row(rows_b, "g_ckv", RB_CKV, 1, rows_b_in)
            load_start(2)
            load_x(2)
            load_start(3)
            load_x(3)
            for j in range(4, 2 * KD):
                load_start(j)
            load_tile(0, 0, 0, first=True)
            sp.dma_start(pos_i[:, :], ins["positions"][0].rearrange("(t p) -> p t", p=P),
                         allow_slow_non_contiguous=True).then_inc(pos_in, 16)
            load_tile(0, 0, 1, first=True)
            load_tile(0, 1, 0)
            with sp.Fori(1, 8) as i:
                load_tile(0, i, 1)
                for k in range(4):
                    load_ada(i + 1, k)
                load_tile(0, i + 1, 0)
                for k in range(4, KD):
                    load_ada(i + 1, k)
            with sp.Fori(8, KF // 2 - 1) as i:
                load_tile(0, i, 1)
                load_tile(0, i + 1, 0)
            load_tile(0, KF // 2 - 1, 1)

            def load_dn(d):
                n0, nch = DN_BASE[d], DN_CHUNKS[d]
                for hf in range(2):
                    base = n0 + hf * nch
                    with sp.Fori(0, nch // 4) as i:
                        for j in range(4):
                            slot_free(i * 4 + (base + j))
                            load(base + j, w_raw[:, (base + j) % RING, :],
                                 w_dn[d][bass.ds(i * (4 * P) + j * P, P), :])
                    for c in range(nch // 4 * 4, nch):
                        slot_free(base + c)
                        load(base + c, w_raw[:, (base + c) % RING, :], w_dn[d][c * P:(c + 1) * P, :])

            load_dn(0)
            for b in range(KD // 2):
                n = N_LAT + b
                slot_free(n)
                load(n, w_raw[:, n % RING, 0:2 * LAT].rearrange("p (k f) -> p k f", k=2),
                     w_in[:, 2 * b:2 * b + 2, 0:LAT])
            slot_free(N_KV)
            load(N_KV, w_raw[:, N_KV % RING, :], ins["w_ukv"][0])
            for b in range(QL // P):
                n = N_UQ + b
                slot_free(n)
                load(n, w_raw[:, n % RING, 0:HM * HE], ins["w_uq"][0, b * P:(b + 1) * P, :])
            dil = w_in[:, :, OFF_DIL:OFF_GATE].rearrange("p k (m g e) -> p k m g e", m=3, g=G)
            for k in range(KD):
                n = N_D0 + k
                slot_free(n)
                load(n, w_raw[:, n % RING, 0:3 * GW].rearrange("p (m e) -> p m e", m=3), dil[:, k, :, 0, :])
            for k in range(KD):
                n = N_D12 + k
                slot_free(n)
                load(n, w_raw[:, n % RING, :].rearrange("p (m e) -> p m e", m=2),
                     w_in[:, k, OFF_DIL + GW:OFF_DIL + 7 * GW].rearrange("p (m e) -> p m e", m=2)[:, :, 0:2 * GW])
            for b in range(KD // 2):
                n = N_V12 + b
                slot_free(n)
                load(n, w_raw[:, n % RING, :].rearrange("p (k f) -> p k f", k=2),
                     w_in[:, 2 * b:2 * b + 2, OFF_DIL + 7 * GW:OFF_GATE])
            for hf in range(2):
                n = N_MRG + hf * MRG
                cols = slice(hf * T, (hf + 1) * T)
                srcs = [w_in[:, 2 * b:2 * b + 2, OFF_GATE + m * D + hf * T:OFF_GATE + m * D + (hf + 1) * T]
                        for m in range(2) for b in range(KD // 2)]
                srcs += [ins["w_o_mla"][0, 2 * b * P:(2 * b + 2) * P, cols].rearrange("(k p) f -> p k f", p=P)
                         for b in range(2)]
                srcs += [ins["w_o_dil"][0, :, cols].rearrange("(k p) f -> p k f", p=P)]
                for src in srcs:
                    slot_free(n)
                    load(n, w_raw[:, n % RING, :].rearrange("p (k f) -> p k f", k=2), src)
                    n += 1
            load_dn(1)
            with sp.Fori(0, KF // 2) as i:
                load_tile(1, i, 0)
                load_tile(1, i, 1)
            load_dn(2)
            for t in range(KT):
                sp.wait_ge(x_new, 8 + t + 1)
                sp.dma_start(out[0, t * P:(t + 1) * P, :], x[:, t, :]).then_inc(out_written, 16)
            sp.wait_ge(out_written, 16 * KT)

        @block.gpsimd
        def _(pool):
            own = Steps(pool, pool_own)
            own.mark(pool.memset(ident[:, :], 0.0))
            own.mark(pool.memset(residue[:, :], 0.0))
            own.mark(pool.memset(mask0[:, :, :], 0.0))
            own.mark(pool.memset(mask12[:, :, :], 0.0))
            own.mark(pool.memset(neg_half[:, :], -0.5))
            for base, n, dim, theta in ((0, MM, ROPE, 10000.0), (MM, MP, RP, 500000.0)):
                for j in range(n):
                    f = np.float32(theta) ** (-np.float32(2 * j) / np.float32(dim))
                    own.mark(pool.memset(inv_freq[:, base + j:base + j + 1], float(f)))
            own.settle()
            pool.affine_select(out=ident[:, :], in_=ident[:, :], compare_op=ALU.not_equal, fill=1.0,
                               base=0, pattern=[[-1, P]], channel_multiplier=1).then_inc(consts_ready, 1)

            last = []

            def rms(n, src, dst, signal, count):
                if last:
                    pool.wait_ge(*last)
                own.mark(pool.tensor_scalar(st_eps[:, 0:n], src, EPS, None, ALU.add))
                own.settle()
                pool.tensor_tensor(dst, st_eps[:, 0:n], neg_half[:, 0:n], ALU.pow).then_inc(signal, 1)
                last[:] = [signal, count]

            def rms_y(m):
                pool.wait_ge(y_squared, m + 1)
                rms(1, st_y[:, m:m + 1], st_yr[:, m:m + 1], y_rms, m + 1)

            def rms_x(m):
                pool.wait_ge(x_squared, m + 1)
                rms(1, st_x[:, m:m + 1], st_xr[:, m:m + 1], x_rms, m + 1)

            for t in range(KT):
                rms_x(t)
            own.settle()
            own.mark(pool.affine_select(
                out=residue[0:DIL, :].rearrange("p (m a) -> p m a", a=DIL),
                in_=residue[0:DIL, :].rearrange("p (m a) -> p m a", a=DIL), compare_op=ALU.not_equal,
                fill=1.0, base=0, pattern=[[0, P // DIL], [-1, DIL]], channel_multiplier=1))
            own.settle()
            pool.memset(st_eps[:, 7:8], 0.0).then_inc(residue_ready, 1)
            for m, pat, base in ((mask0[:, :, :], [[P, 3], [1, P]], -P), (mask12[:, 0, :], [[1, P]], 0)):
                own.mark(pool.affine_select(out=m, in_=m, compare_op=ALU.is_ge, fill=MASKED,
                                            base=base + E, pattern=pat, channel_multiplier=-1))
                own.settle()
                own.mark(pool.affine_select(out=m, in_=m, compare_op=ALU.is_ge, fill=MASKED, base=E - base,
                                            pattern=[[-a, b] for a, b in pat], channel_multiplier=1))
                own.settle()
            pool.memset(st_eps[:, 6:7], 0.0).then_inc(masks_ready, 1)

            def post(d, tiles):
                for t in tiles:
                    rms_y(4 * d + t)
                if d < 2:
                    for t in tiles:
                        rms_x(4 * (d + 1) + t)

            post(0, (0, 1))
            post(0, (2, 3))
            for t in range(KT):
                pool.wait_ge(lat_squared, 2 * (t + 1))
                rms(2, st_lat[:, t, :], st_latr[:, t, :], lat_rms, t + 1)
            pool.wait_ge(w_used, N_D0 + 1)
            for z in (kz_hi, kz_lo):
                for a in range(2):
                    pool.memset(z[(1 - a) * E:(1 - a) * E + E, :, a, :].bitcast(F32), 0.0).then_inc(kz_clear, 1)
            post(1, (0, 1))
            post(1, (2, 3))
            post(2, (0, 1))
            post(2, (2, 3))

        @block.scalar
        def _(act):
            copy, square = ACT.Copy, ACT.Square
            split = [0]
            junk_last = []

            def split_block(n, s_n):
                slot = s_n % RING
                act.wait_ge(raw_in[slot], n * (16 // RING) + (16 - 16 // RING * slot))
                if s_n >= RING and s_n != N_KV:
                    act.wait_ge(w_used, n - (RING - 1))
                width = w_shape(s_n)
                dst = ukv_hi[:, :] if s_n == N_KV else w_hi[:, slot, 0:width]
                act.activation(dst, w_raw[:, slot, 0:width], copy).then_inc(hi_ready, 1)

            def split_to(n):
                while split[0] <= min(n, N_END - 1):
                    split_block(split[0], split[0])
                    split[0] += 1

            def split_a(d, hf, c, s_c):
                src = m_t if d == 1 else a_buf
                slot = (hf * DN_CHUNKS[d] + s_c) % RING
                if hf or s_c >= RING:
                    act.wait_ge(w_used, c + (DN_BASE[d] + hf * DN_CHUNKS[d] - RING + 1))
                if d == 1:
                    act.wait_ge(m_t_ready, c + 1)
                act.activation(a_hi[:, slot, :], src[:, bass.ds(c * T + hf * 256, 256)], copy)\
                    .then_inc(a_hi_ready, 1)

            def squares(src, dst, signal, count):
                if junk_last:
                    act.wait_ge(*junk_last)
                act.activation(junk[:, :], src, square, scale=float(D) ** -0.5, accum_out=dst).then_inc(signal, 1)
                junk_last[:] = [signal, count]

            def sq_y(m):
                d, t = m // 4, m % 4
                if t == 2:
                    act.wait_ge(third_summed, d + 1)
                else:
                    act.wait_ge(w_used, DN_BASE[d] + (t // 2 + 1) * DN_CHUNKS[d])
                b = y_bank(d, t)
                squares(ps[:, b:b + 2, :].rearrange("p a b -> p (a b)"), st_y[:, m:m + 1], y_squared, m + 1)

            def sq_x(m):
                s, t = m // 4, m % 4
                if s:
                    act.wait_ge(x_new, m - 4 + 1)
                else:
                    act.wait_ge(x_in[t], 16)
                squares(x[:, t, :], st_x[:, m:m + 1], x_squared, m + 1)

            def modulated_upper(m):
                s, t = m // 4, m % 4
                act.wait_ge(x_turned, m + 1)
                if s == 0:
                    act.wait_ge(first_scale_ready, 1)
                if m >= 2:
                    act.wait_ge(h_hi_ready, m - 1)
                    act.wait_ge(h_ready, m - 1)
                for c in range(KD // 2, KD):
                    i = act.activation(h32[:, m % 2, c, :], ps[:, x_bank(s, t) + 1, c % 4 * P:(c % 4 + 1) * P],
                                       ACT.Identity, scale=scale_col[:, s, c:c + 1], bias=ada_col[:, 3 * s, c:c + 1])
                i.then_inc(h32_upper_ready, 1)

            def h_high(m):
                t = m % 4
                act.wait_ge(h32_ready, m + 1)
                act.wait_ge(h32_upper_ready, m + 1)
                act.activation(h_hi[:, :, t * P:(t + 1) * P], h32[:, m % 2, :, :], copy).then_inc(h_hi_ready, 1)

            def gain_row(s):
                act.wait_ge(g_spread, s + 1)
                b = G_BANK[s]
                act.activation(g_row[:, :], ps[:, b:b + 2, :].rearrange("p a b -> p (a b)"), copy)\
                    .then_inc(g_ready, 1)

            def gate_up(g):
                n0, f0 = GU_BASE[g], KF * g

                def tile(i, q, straight):
                    n = n0 + 2 * q + 2
                    if straight:
                        split_to(n + 4 * i + 1)
                    else:
                        split_block(i * 4 + n, n + 4)
                        split_block(i * 4 + (n + 1), n + 5)
                    act.wait_ge(w_used, i * 4 + (n0 + 2 * q + 2))
                    if not (straight and i == 0):
                        act.wait_ge(a_ready, i * 2 + (f0 + q - 1))
                    act.activation(silu[:, q, :], ps[:, 4 + 2 * q, :], ACT.Silu).then_inc(silu_done, 1)

                for q in range(2):
                    tile(0, q, True)
                for lo, hi in ((1, 8), (8, KF // 2 - 1)):
                    with act.Fori(lo, hi) as i:
                        for q in range(2):
                            tile(i, q, False)
                gain_row(2 * g)
                split[0] = n0 + 2 * KF - 4 + LEAD
                tile(KF // 2 - 1, 0, True)
                act.wait_ge(a_ready, f0 + LEAD)
                for c in range(LEAD):
                    split_a(2 * g, 0, c, c)
                tile(KF // 2 - 1, 1, True)

            def down_chunk(d, hf, c):
                nch = DN_CHUNKS[d]
                split_to(DN_BASE[d] + hf * nch + c + LEAD)
                if c + LEAD < nch:
                    split_a(d, hf, c + LEAD, c + LEAD)
                elif hf == 0:
                    split_a(d, 1, c + LEAD - nch, c + LEAD - nch)

            def down(d):
                nch, n0 = DN_CHUNKS[d], DN_BASE[d]

                def chunk_loop(hf, first, last):
                    base = n0 + hf * nch
                    with act.Fori(0, (last - first) // 4) as i:
                        for j in range(first, first + 4):
                            split_block(i * 4 + (base + j + LEAD), base + j + LEAD)
                            split_a(d, hf, i * 4 + (j + LEAD), j + LEAD)
                    split[0] = base + last + LEAD

                if nch > 8:
                    act.wait_ge(a_ready, KF * (1 + d // 2))
                    for c in range(4):
                        down_chunk(d, 0, c)
                    chunk_loop(0, 4, 20)
                    down_chunk(d, 0, 20)
                    down_chunk(d, 0, 21)
                else:
                    for c in range(2, nch):
                        down_chunk(d, 0, c)
                        if c == 4:
                            gain_row(1)
                m = 4 * (d + 1)
                for c in range(8):
                    down_chunk(d, 1, c)
                    if c == 0:
                        sq_y(4 * d)
                        sq_y(4 * d + 1)
                    if d < 2 and c == 2:
                        sq_x(m)
                    if d < 2 and c == 3:
                        sq_x(m + 1)
                    if d < 2 and c == 5:
                        modulated_upper(m)
                    if d < 2 and c == 6:
                        modulated_upper(m + 1)
                        h_high(m)
                    if d < 2 and c == 7:
                        h_high(m + 1)
                if nch > 8:
                    chunk_loop(1, 8, 20)
                    down_chunk(d, 1, 20)
                    down_chunk(d, 1, 21)
                sq_y(4 * d + 2)
                sq_y(4 * d + 3)
                split_to(n0 + 2 * nch + 2)
                if d < 2:
                    sq_x(m + 2)
                split_to(n0 + 2 * nch + 3)
                if d < 2:
                    sq_x(m + 3)
                    for t in (2, 3):
                        modulated_upper(m + t)
                    for t in (2, 3):
                        h_high(m + t)

            act.wait_ge(rows_turned, 1)
            act.activation(col_a[:, :], ps[:, 0, 0:RA_N], copy).then_inc(cols_ready, 1)
            act.wait_ge(cols_ready, 1)
            act.activation(cond[:, :], col_a[:, RA_C:RA_C + KD], ACT.Silu).then_inc(cond_ready, 1)
            for t in range(KT):
                sq_x(t)
            act.wait_ge(rows_turned, 2)
            act.activation(col_b[:, :], ps[:, 1, 0:RB_N], copy).then_inc(cols_ready, 1)
            split_to(1)
            for t in (0, 2):
                modulated_upper(t)
                modulated_upper(t + 1)
                h_high(t)
                h_high(t + 1)
                split_to(3)
            act.wait_ge(sins_ready, 1)
            act.activation(sin_t[:, :, :], ang[:, 1, :, :], ACT.Sin).then_inc(trig_ready, 1)
            act.activation(cos_t[:, :, :], ang[:, 2, :, :], ACT.Sin).then_inc(trig_ready, 1)
            gate_up(0)
            down(0)

            def latents(tiles):
                for t in tiles:
                    if t == KT - 1:
                        act.wait_ge(w_used, N_LAT + KD // 2)
                    else:
                        act.wait_ge(lat_summed, 1 + t // 2)
                    act.activation(lat[:, t, :], ps[:, t, 0:LAT], copy).then_inc(lat_copied, 1)
                for t in tiles:
                    act.wait_ge(lat_copied, t + 1)
                    for c, (a, b) in enumerate(((0, QL), (QL, QL + KVL))):
                        act.activation(c_t[:, a // P:b // P, t * P:(t + 1) * P],
                                       lat[:, t, a:b].rearrange("p (c n) -> p c n", n=P), square,
                                       scale=float(b - a) ** -0.5, accum_out=st_lat[:, t, c:c + 1])\
                            .then_inc(lat_squared, 1)

            def latents_high(half):
                tiles, tokens = slice(2 * half, 2 * half + 2), slice(half * 256, half * 256 + 256)
                act.wait_ge(lat_turned, 2 * half + 2)
                act.wait_ge(c_t_ready, 2 * half + 2)
                for z in range(2):
                    act.activation(mk_hi[NOPE:HE, z, tokens].rearrange("p (t n) -> p t n", t=2),
                                   ps[NOPE:HE, tiles, 3 * P:4 * P], copy).then_inc(krot_hi, 1)
                act.activation(c_hi[:, :, tokens], c_t[:, :, tokens], copy).then_inc(c_hi_ready, 1)

            def values_high(half):
                for t in (2 * half, 2 * half + 1):
                    if t < KT - 1:
                        act.wait_ge(mv_done, t + 1)
                    else:
                        act.wait_ge(w_used, N_KV + 1)
                    act.activation(mv_hi[:, t, :], ps[:, 4 + t % 2, :], copy).then_inc(mv_hi_ready, 1)

            def queries(half):
                for t in (2 * half, 2 * half + 1):
                    if t < KT - 1:
                        act.wait_ge(uq_done, t + 1)
                    else:
                        act.wait_ge(w_used, N_UQ + 2)
                    b = UQ_BANK[t]
                    act.activation(q_nat[:, t, :].rearrange("p (a b) -> p a b", a=2), ps[:, b:b + 2, 0:384],
                                   copy).then_inc(q_copied, 1)

            latents((0, 1))
            split_to(N_KV)
            latents_high(0)
            latents((2,))
            split_to(N_UQ + 1)
            latents((3,))
            values_high(0)
            queries(0)
            latents_high(1)
            values_high(1)
            queries(1)

            def m_query(h):
                z = h % 2
                act.wait_ge(m_turned, h + 1)
                if h >= 2:
                    act.wait_ge(m_scores, KT * (h - 1))
                act.activation(mq_hi[0:HE, z, :], ps[0:HE, 0, :], copy, scale=MLA_SCALE).then_inc(m_qk_hi, 1)

            def m_key(h):
                z = h % 2
                act.activation(mk_hi[0:NOPE, z, :], ps[0:NOPE, 1, :], copy).then_inc(m_qk_hi, 1)

            def m_out_copy(h):
                act.wait_ge(m_pv, 2 * h + 2)
                a = h % 2 * VD
                act.activation(o_mla[a:a + VD, h // 2, :], ps[a:a + VD, 7, :], copy).then_inc(m_out_copied, 1)

            m_query(0)
            m_key(0)
            for u in range(MU + 4):
                if u % KT == 1 and u // KT + 1 < HM:
                    m_query(u // KT + 1)
                    m_key(u // KT + 1)
                v = u - 3
                if 0 <= v < MU:
                    act.wait_ge(m_pt_done, v + 1)
                    if v >= 4:
                        act.wait_ge(m_pv, v // 2 - 1)
                    act.activation(mpt_hi[:, v // 2 % 2, :, v % 2 * P:v % 2 * P + P],
                                   ps[:, 5 + v % 2, :].rearrange("p (c n) -> p c n", c=KT), copy)\
                        .then_inc(m_pt_hi, 1)
                if u < MU:
                    act.wait_ge(m_max, u + 1)
                    if u >= 3:
                        act.wait_ge(m_pt_done, u - 2)
                    act.activation(mp[:, u % 3, :], ps[:, 2 + u % 3, :], ACT.Exp, bias=mla_nm[:, u:u + 1],
                                   accum_out=mla_z[:, u:u + 1]).then_inc(m_exp, 1)
                if u in (11, 15, 19, 23):
                    split_to(N_D0 + u // KT - 2)
                if u >= 8 and u % KT == 0:
                    m_out_copy(u // KT - 2)
            m_out_copy(HM - 1)

            split_to(N_D0 + 10)
            act.wait_ge(w_used, N_D0 + KD)
            for t in range(KT):
                act.activation(qk0[:, t, :], ps[:, 2 * t, :], copy).then_inc(d0_copied, 1)
                act.activation(v0_hi[:, t, :], ps[:, 2 * t + 1, 0:GW], copy).then_inc(v0_hi_ready, 1)
            split_to(N_V12 + 2)
            act.wait_ge(w_used, N_D12 + KD)

            def d12_copy(t):
                act.activation(qk12[:, t, :, :], ps[:, 2 * t:2 * t + 2, :], copy).then_inc(d12_copied, 1)

            d12_copy(0)
            d12_copy(1)

            def d_operands(i):
                kind, g, _, bank, before = PREP[i]
                act.wait_ge(d_turned, i + 1)
                if before:
                    act.wait_ge(d_scores, before)
                if i == 0:
                    act.wait_ge(kz_clear, 4)
                parts = [(dq_hi[:, g, :], ps[:, bank, :], DIL_SCALE)]
                parts += [(kz_hi[a * E:a * E + E, g, a, :], ps[a * E:a * E + E, bank + 1, :], 1.0) for a in range(2)]
                for dst, src, scale in parts:
                    if kind == "strided":
                        dst = dst.rearrange("p (r l) -> p r l", r=DIL)
                        src = src.rearrange("p (l r) -> p r l", r=DIL)
                    act.activation(dst, src, copy, scale=scale).then_inc(d_qk_hi, 1)

            def d_exp_unit(v):
                kind, p, a, t = D_UNITS[v]
                s = v % 3
                act.wait_ge(d_max, v + 1)
                if kind == "local":
                    w = len(chunks(t)) * P
                    act.activation(dp[:, s, 0:w], dp[:, s, 0:w], ACT.Exp, bias=dil_nm[:, 0, p, t, a:a + 1],
                                   accum_out=dil_z[:, 0, p, t, a:a + 1]).then_inc(d_exp, 1)
                else:
                    view = dp[:, s, :].rearrange("p (g a n) -> p a g n", g=2, a=2)
                    for b in range(2):
                        act.activation(view[:, b, :, :], view[:, b, :, :], ACT.Exp,
                                       bias=dil_nm[:, 1, p, t, b:b + 1],
                                       accum_out=dil_z[:, 1, p, t, b:b + 1]).then_inc(d_exp, 1)

            def d_pt_high(v):
                act.wait_ge(d_pt_done, v + 1)
                sem_, value = pt_free(v)
                if value:
                    act.wait_ge(sem_, value)
                act.activation(pt_view(dpt_hi, v), pt_bank(v), copy).then_inc(d_pt_hi, 1)

            def u_copy(i):
                if i < 4:
                    act.wait_ge(pv0_used, KT * (i + 1))
                    p, a = i // 2, i % 2
                    act.activation(u0[a * E:a * E + E, p, :], ps[a * E:a * E + E, 7, :], copy).then_inc(u_copied, 1)
                    return
                act.wait_ge(pv12_used, i - 3)
                p, r = (i - 4) // KT, (i - 4) % KT
                for a in range(2):
                    c = r % 2 * 256 + a * P
                    o = u12[a * E:a * E + E, p, :].rearrange("p (l r) -> p r l", r=DIL)[:, r, :]
                    act.activation(o, ps[a * E:a * E + E, 7, c:c + P], copy).then_inc(u_copied, 1)

            d_operands(0)
            d12_copy(2)
            d12_copy(3)
            split_to(N_V12 + 3)
            for v in range(len(D_UNITS) + 5):
                if 0 <= v - 3 < len(D_UNITS):
                    d_pt_high(v - 3)
                for i in PREP_AT.get(v, ()):
                    d_operands(i)
                if v < len(D_UNITS):
                    d_exp_unit(v)
                for r in V12_COPIES.get(v, ()):
                    if r < 2:
                        act.wait_ge(v12_half, 1)
                    else:
                        act.wait_ge(w_used, N_V12 + 4)
                    act.activation(v12(r)[0], ps[:, r % 2, :], copy).then_inc(v12_hi_ready, 1)
                if v in (8, 12, 16, 20):
                    u_copy(v // KT - 2)
                if v - 5 >= N_LOCAL:
                    u_copy(v - 5 - N_LOCAL + 4)
                if 24 <= v < 28:
                    split_to(N_MRG + v - 24)

            for p in range(2):
                act.wait_ge(mix_spread, p + 1)
                for j in range(4):
                    o, i_ = mix[:, p, j, :], ps[:, 4 * p + j, :]
                    if j >= 2:
                        o = o.rearrange("p (l r) -> p r l", r=DIL)
                        i_ = i_.rearrange("p (r l) -> p r l", r=DIL)
                    act.activation(o, i_, copy).then_inc(mix_copied, 1)
            act.activation(om_hi[:, :, :], o_mla[:, :, :], copy).then_inc(om_hi_ready, 1)

            def merged_copy(hf):
                for c in range(4):
                    act.wait_ge(m_t_done, 4 * hf + c + 1)
                    act.activation(m_t[:, (4 * hf + c) * T:(4 * hf + c + 1) * T], ps[:, c, :], copy)\
                        .then_inc(m_t_ready, 1)

            for hf in range(2):
                n = N_MRG + hf * MRG
                ga, gb, om, od = M_BANKS[hf]
                if hf == 0:
                    split_to(n + 6)
                    for p in range(2):
                        for j in range(2):
                            act.wait_ge(mix_diff, 2 * p + j + 1)
                            act.activation(mix[:, p, 2 * j, :], mix[:, p, 2 * j, :], ACT.Exp).then_inc(mix_exp, 1)
                else:
                    split_to(n + 4)
                    merged_copy(0)
                split_to(n + 7)
                act.wait_ge(w_used, n + 4)
                if hf:
                    act.wait_ge(m_t_done, 4)
                for t in range(KT):
                    act.activation(sg_a[:, t, :], ps[:, ga + t, :], ACT.Sigmoid).then_inc(ga_ready, 1)
                split_to(n + 10)
                if hf == 0:
                    act.wait_ge(mixed, 2)
                    act.activation(od_hi[:, :, :], u12[:, :, :], copy).then_inc(od_hi_ready, 1)
                act.wait_ge(w_used, n + 8)
                for t in range(KT):
                    act.activation(sg_b[:, t, :], ps[:, gb + t, :], ACT.Sigmoid).then_inc(gb_ready, 1)
                split_to(n + 14 if hf == 0 else n + 13)
            for c in range(LEAD):
                split_a(1, 0, c, c)
            down_chunk(1, 0, 0)
            down_chunk(1, 0, 1)
            merged_copy(1)
            down(1)
            gate_up(1)
            down(2)

        @block.vector
        def _(dve):
            own = Steps(dve, dve_own)
            split = [0]

            def split_block(n, s_n):
                slot = s_n % RING
                dve.wait_ge(hi_ready, n + 1)
                width = w_shape(s_n)
                hi, lo = (ukv_hi[:, :], ukv_lo[:, :]) if s_n == N_KV else \
                    (w_hi[:, slot, 0:width], w_lo[:, slot, 0:width])
                dve.tensor_tensor(lo, w_raw[:, slot, 0:width], hi.bitcast(F32), ALU.subtract).then_inc(lo_ready, 1)

            def split_to(n):
                while split[0] <= min(n, N_END - 1):
                    split_block(split[0], split[0])
                    split[0] += 1

            def split_a(d, hf, c, s_c):
                src = m_t if d == 1 else a_buf
                slot = (hf * DN_CHUNKS[d] + s_c) % RING
                dve.wait_ge(a_hi_ready, c + (DN_COUNT[d] + hf * DN_CHUNKS[d] + 1))
                dve.tensor_tensor(a_lo[:, slot, :], src[:, bass.ds(c * T + hf * 256, 256)],
                                  a_hi[:, slot, :].bitcast(F32), ALU.subtract).then_inc(a_lo_ready, 1)

            def update(m):
                d, t = m // 4, m % 4
                dve.wait_ge(y_rms, m + 1)
                dve.wait_ge(g_ready, d + 1)
                if m:
                    dve.wait_ge(x_new, m)
                b = y_bank(d, t)
                own.mark(dve.scalar_tensor_tensor(upd[:, :], ps[:, b:b + 2, :].rearrange("p a b -> p (a b)"),
                                                  st_yr[:, m:m + 1], g_row[:, :], ALU.mult, ALU.mult))
                own.settle()
                dve.tensor_tensor(x[:, t, :], x[:, t, :], upd[:, :], ALU.add).then_inc(x_new, 1)

            def norm(m):
                dve.wait_ge(x_rms, m + 1)
                if m:
                    dve.wait_ge(x_turned, m)
                dve.tensor_scalar(xn[:, :], x[:, m % 4, :], st_xr[:, m:m + 1], None, ALU.mult).then_inc(xn_ready, 1)

            def modulated(m):
                s, t = m // 4, m % 4
                dve.wait_ge(x_turned, m + 1)
                if m >= 2:
                    dve.wait_ge(h_hi_ready, m - 1)
                    dve.wait_ge(h_ready, m - 1)
                for c in range(KD // 2):
                    src = ps[:, x_bank(s, t), c * P:(c + 1) * P]
                    i = dve.tensor_scalar(h32[:, m % 2, c, :], src, scale_col[:, s, c:c + 1],
                                          ada_col[:, 3 * s, c:c + 1],
                                          ALU.mult, ALU.add)
                i.then_inc(h32_ready, 1)

            def h_low(m):
                t = m % 4
                dve.wait_ge(h_hi_ready, m + 1)
                dve.tensor_tensor(h_lo[:, :, t * P:(t + 1) * P], h32[:, m % 2, :, :],
                                  h_hi[:, :, t * P:(t + 1) * P].bitcast(F32), ALU.subtract).then_inc(h_ready, 1)

            def add_start(v, k):
                j = v * KD + k
                acc = (ada_acc, upd)[v]
                dve.wait_ge(start_in[j], 16)
                if k == 0:
                    dve.tensor_scalar(acc[:, :], start_slot(j), cond[:, k:k + 1], None, ALU.mult)\
                        .then_inc(ada_added, 1)
                else:
                    dve.wait_ge(ada_added, j)
                    dve.scalar_tensor_tensor(acc[:, :], start_slot(j), cond[:, k:k + 1], acc[:, :],
                                             ALU.mult, ALU.add).then_inc(ada_added, 1)

            def add_ada(v, k):
                slot = k % 4
                dve.wait_ge(ada_in[slot], v * 32 + (16 * (k // 4) - 48))
                if k:
                    dve.wait_ge(ada_added, v * KD + k)
                if k == 0:
                    dve.wait_ge(ada_turned, v)
                    dve.tensor_scalar(ada_acc[:, :], ada_raw[:, slot, :], cond[:, k:k + 1], None, ALU.mult)\
                        .then_inc(ada_added, 1)
                else:
                    dve.scalar_tensor_tensor(ada_acc[:, :], ada_raw[:, slot, :], cond[:, k:k + 1], ada_acc[:, :],
                                             ALU.mult, ALU.add).then_inc(ada_added, 1)

            def sum_ada(v):
                dve.wait_ge(ada_turned, v + 1)
                dve.tensor_reduce(ada_col[:, :, :].rearrange("p v c -> p (v c)")[:, bass.ds(v * KD, KD)],
                                  ps[:, 0:2, :].rearrange("p b (c n) -> p (b c) n", n=P), AXIS.X, ALU.add)\
                    .then_inc(ada_summed, 1)

            def gate_up(g):
                n0, f0 = GU_BASE[g], KF * g

                def tile(i, q, straight, ada):
                    n = n0 + 2 * q + 2
                    if straight:
                        split_to(n + 4 * i + 1)
                    else:
                        split_block(i * 4 + n, n + 4)
                        split_block(i * 4 + (n + 1), n + 5)
                    if ada:
                        for k in range(4 * q, 4 * q + 4):
                            add_ada(i + 1, k)
                    dve.wait_ge(silu_done, i * 2 + (f0 + q + 1))
                    dve.tensor_tensor(a_buf[:, bass.ds(i * (2 * T) + q * T, T)], silu[:, q, :], ps[:, 5 + 2 * q, :],
                                      ALU.mult).then_inc(a_ready, 1)

                for q in range(2):
                    tile(0, q, True, False)
                with dve.Fori(1, 8) as i:
                    for q in range(2):
                        tile(i, q, False, g == 0)
                    if g == 0:
                        sum_ada(i + 1)
                if g == 0:
                    modulation()
                with dve.Fori(8, KF // 2 - 1) as i:
                    for q in range(2):
                        tile(i, q, False, False)
                split[0] = n0 + 2 * KF - 4 + LEAD
                tile(KF // 2 - 1, 0, True, False)
                dve.wait_ge(a_ready, f0 + LEAD)
                for c in range(LEAD):
                    split_a(2 * g, 0, c, c)
                tile(KF // 2 - 1, 1, True, False)

            def modulation():
                dve.wait_ge(ada_summed, 9)
                own.mark(dve.tensor_tensor(ada_col[:, 2:9, :], ada_col[:, 2:9, :],
                                           col_a[:, RA_B + 2 * KD:RA_B + 9 * KD].rearrange("p (v c) -> p v c", c=KD),
                                           ALU.add))
                own.settle()
                for s in range(3):
                    if s:
                        own.mark(dve.scalar_tensor_tensor(
                            scale_col[:, s, :], ada_col[:, 3 * s + 1, :], 1.0,
                            col_a[:, RA_G + s * KD:RA_G + (s + 1) * KD], ALU.add, ALU.mult))
                    dve.scalar_tensor_tensor(gate_col[:, s, :], ada_col[:, 3 * s + 2, :], 1.0 if s == 1 else 0.5,
                                             col_b[:, RB_GP + s * KD:RB_GP + (s + 1) * KD], ALU.mult, ALU.mult)\
                        .then_inc(gates_ready, 1)

            def down_chunk(d, hf, c):
                nch = DN_CHUNKS[d]
                split_to(DN_BASE[d] + hf * nch + c + LEAD)
                if c + LEAD < nch:
                    split_a(d, hf, c + LEAD, c + LEAD)
                elif hf == 0:
                    split_a(d, 1, c + LEAD - nch, c + LEAD - nch)

            def down(d):
                nch, n0 = DN_CHUNKS[d], DN_BASE[d]

                def chunk_loop(hf, first, last):
                    base = n0 + hf * nch
                    with dve.Fori(0, (last - first) // 4) as i:
                        for j in range(first, first + 4):
                            split_block(i * 4 + (base + j + LEAD), base + j + LEAD)
                            split_a(d, hf, i * 4 + (j + LEAD), j + LEAD)
                    split[0] = base + last + LEAD

                if nch > 8:
                    dve.wait_ge(a_ready, KF * (1 + d // 2))
                    for c in range(4):
                        down_chunk(d, 0, c)
                    chunk_loop(0, 4, 20)
                    down_chunk(d, 0, 20)
                    down_chunk(d, 0, 21)
                else:
                    for c in range(2, nch):
                        down_chunk(d, 0, c)
                m = 4 * (d + 1)
                for c in range(8):
                    down_chunk(d, 1, c)
                    if c == 1:
                        update(4 * d)
                    if c == 2:
                        update(4 * d + 1)
                    if d < 2:
                        if c == 3:
                            norm(m)
                        if c == 4:
                            norm(m + 1)
                        if c == 5:
                            modulated(m)
                        if c == 6:
                            modulated(m + 1)
                            h_low(m)
                        if c == 7:
                            h_low(m + 1)
                if nch > 8:
                    chunk_loop(1, 8, 20)
                    down_chunk(d, 1, 20)
                    down_chunk(d, 1, 21)
                update(4 * d + 2)
                split_to(n0 + 2 * nch + 2)
                update(4 * d + 3)
                split_to(n0 + 2 * nch + 3)
                if d < 2:
                    norm(m + 2)
                    norm(m + 3)
                    modulated(m + 2)
                    modulated(m + 3)
                    h_low(m + 2)
                    h_low(m + 3)

            dve.wait_ge(cond_ready, 1)
            for k in range(KD):
                add_start(0, k)
                if k < KT:
                    norm(k)
            for k in range(KD):
                add_start(1, k)
                if k == 1:
                    sum_ada(0)
            sum_ada(1)
            dve.wait_ge(ada_summed, 2)
            dve.wait_ge(cols_ready, 2)
            own.mark(dve.tensor_tensor(ada_col[:, 0:2, :], ada_col[:, 0:2, :],
                                       col_a[:, RA_B:RA_B + 2 * KD].rearrange("p (v c) -> p v c", c=KD), ALU.add))
            own.settle()
            dve.scalar_tensor_tensor(scale_col[:, 0, :], ada_col[:, 1, :], 1.0, col_a[:, RA_G:RA_G + KD],
                                     ALU.add, ALU.mult).then_inc(first_scale_ready, 1)
            dve.wait_ge(first_scale_ready, 1)
            for t in (0, 2):
                modulated(t)
                modulated(t + 1)
                if t == 0:
                    split_to(0)
                h_low(t)
                h_low(t + 1)
                split_to(3)
            dve.wait_ge(pos_in, 16)
            own.mark(dve.tensor_copy(pos_f[:, :], pos_i[:, :]))
            own.settle()
            dve.wait_ge(consts_ready, 1)
            shape = [P, KT, MM + MP]
            own.mark(dve.tensor_tensor(ang[:, 0, :, :], pos_f[:, :].unsqueeze(2).broadcast_to(shape),
                                       inv_freq[:, :].unsqueeze(1).broadcast_to(shape), ALU.mult))
            own.settle()
            magic = 1.5 * 2.0 ** 23
            own.mark(dve.tensor_scalar(ang[:, 1, :, :], ang[:, 0, :, :], 1.0 / (2.0 * math.pi), None, ALU.mult))
            own.settle()
            own.mark(dve.tensor_scalar(ang[:, 2, :, :], ang[:, 1, :, :], magic, None, ALU.add))
            own.settle()
            own.mark(dve.tensor_scalar(ang[:, 3, :, :], ang[:, 2, :, :], magic, None, ALU.subtract))
            own.settle()
            turn1 = 6.28125
            turn2 = float(np.float32(math.floor((2 * math.pi - turn1) * 2 ** 21) / 2 ** 21))
            turn3 = float(np.float32(2 * math.pi - turn1 - turn2))
            a, b = 0, 1
            for part in (turn1, turn2, turn3):
                own.mark(dve.scalar_tensor_tensor(ang[:, b, :, :], ang[:, 3, :, :], -part, ang[:, a, :, :],
                                                  ALU.mult, ALU.add))
                own.settle()
                a, b = b, a
            limit = 3.1415925
            own.mark(dve.tensor_scalar(ang[:, a, :, :], ang[:, a, :, :], limit, -limit, ALU.min, ALU.max))
            own.settle()
            assert a == 1
            own.mark(dve.scalar_tensor_tensor(ang[:, 3, :, :], ang[:, 1, :, :], -1.0, ang[:, 1, :, :],
                                              ALU.mult, ALU.min))
            own.settle()
            dve.tensor_scalar(ang[:, 2, :, :], ang[:, 3, :, :], math.pi / 2, None, ALU.add).then_inc(sins_ready, 1)
            dve.wait_ge(residue_mult, 1)
            dve.wait_ge(masks_ready, 1)
            own.mark(dve.tensor_scalar(mask12[:, 1, :], ps[:, 2, 0:P], 1.0, -MASKED, ALU.subtract, ALU.mult))
            gate_up(0)
            down(0)

            def rotate(t1, t2, c, s, tmp, signal):
                own.mark(dve.tensor_tensor(tmp[0], t1, c, ALU.mult))
                own.mark(dve.tensor_tensor(tmp[1], t2, s, ALU.mult))
                own.mark(dve.tensor_tensor(tmp[2], t2, c, ALU.mult))
                own.mark(dve.tensor_tensor(tmp[3], t1, s, ALU.mult))
                own.settle()
                own.mark(dve.tensor_tensor(t1, tmp[0], tmp[1], ALU.subtract))
                dve.tensor_tensor(t2, tmp[2], tmp[3], ALU.add).then_inc(signal, 1)

            cos_m, sin_m = cos_t[:, :, 0:MM], sin_t[:, :, 0:MM]
            cos_p, sin_p = cos_t[:, :, MM:MM + MP], sin_t[:, :, MM:MM + MP]
            gains = col_b[:, RB_CQ:RB_CQ + 3].unsqueeze(2).broadcast_to([P, 3, P])
            qv = q_nat[:, :, :].rearrange("p t (h e) -> p t h e", e=HE)

            def latents(tiles):
                for t in tiles:
                    dve.wait_ge(lat_rms, t + 1)
                    own.mark(dve.tensor_scalar(lat[:, t, 0:QL], lat[:, t, 0:QL], st_latr[:, t, 0:1], None, ALU.mult))
                    dve.tensor_scalar(lat[:, t, QL:QL + KVL], lat[:, t, QL:QL + KVL], st_latr[:, t, 1:2], None,
                                      ALU.mult).then_inc(lat_normed, 1)

            def rotate_key(half):
                tiles = slice(2 * half, 2 * half + 2)
                dve.wait_ge(lat_copied, 2 * half + 2)
                t1, t2 = lat[:, tiles, QL + KVL:QL + KVL + MM], lat[:, tiles, QL + KVL + MM:LAT]
                tmp = [rot_m[:, j, half * 2 * MM:(half + 1) * 2 * MM].rearrange("p (t e) -> p t e", t=2)
                       for j in range(4)]
                own.mark(dve.tensor_tensor(tmp[0], t1, cos_m[:, tiles, :], ALU.mult))
                own.mark(dve.tensor_tensor(tmp[1], t2, sin_m[:, tiles, :], ALU.mult))
                own.mark(dve.tensor_tensor(tmp[2], t2, cos_m[:, tiles, :], ALU.mult))
                own.mark(dve.tensor_tensor(tmp[3], t1, sin_m[:, tiles, :], ALU.mult))
                own.settle()
                own.mark(dve.tensor_tensor(k_rot[:, tiles, NOPE:NOPE + MM], tmp[0], tmp[1], ALU.subtract))
                dve.tensor_tensor(k_rot[:, tiles, NOPE + MM:HE], tmp[2], tmp[3], ALU.add).then_inc(krot_turned, 1)

            def latents_gain(half):
                for t in (2 * half, 2 * half + 1):
                    dve.wait_ge(lat_turned, t + 1)
                    dve.tensor_tensor(c_t[:, :, t * P:(t + 1) * P],
                                      ps[:, t, 0:3 * P].rearrange("p (c n) -> p c n", n=P), gains, ALU.mult)\
                        .then_inc(c_t_ready, 1)

            def latents_low(half):
                tiles, tokens = slice(2 * half, 2 * half + 2), slice(half * 256, half * 256 + 256)
                dve.wait_ge(krot_hi, 2 * half + 2)
                for z in range(2):
                    dve.tensor_tensor(mk_lo[NOPE:HE, z, tokens].rearrange("p (t n) -> p t n", t=2),
                                      ps[NOPE:HE, tiles, 3 * P:4 * P],
                                      mk_hi[NOPE:HE, z, tokens].rearrange("p (t n) -> p t n", t=2).bitcast(F32),
                                      ALU.subtract).then_inc(krot_ready, 1)
                dve.wait_ge(c_hi_ready, half + 1)
                dve.wait_ge(c_t_ready, 2 * half + 2)
                dve.tensor_tensor(c_lo[:, :, tokens], c_t[:, :, tokens], c_hi[:, :, tokens].bitcast(F32),
                                  ALU.subtract).then_inc(c_ready, 1)

            def values_low(half):
                for t in (2 * half, 2 * half + 1):
                    dve.wait_ge(mv_hi_ready, t + 1)
                    dve.tensor_tensor(mv_lo[:, t, :], ps[:, 4 + t % 2, :], mv_hi[:, t, :].bitcast(F32),
                                      ALU.subtract).then_inc(mv_ready, 1)

            def queries(half):
                tiles = slice(2 * half, 2 * half + 2)
                wide = [P, 2, HM, MM]
                dve.wait_ge(q_copied, 2 * half + 2)
                rotate(qv[:, tiles, :, NOPE:NOPE + MM], qv[:, tiles, :, NOPE + MM:HE],
                       cos_m[:, tiles, :].unsqueeze(2).broadcast_to(wide),
                       sin_m[:, tiles, :].unsqueeze(2).broadcast_to(wide),
                       [rot_m[:, j, half * 256:half * 256 + 256].rearrange("p (t h e) -> p t h e", t=2, h=HM)
                        for j in range(4)], q_rotated)

            dve.wait_ge(trig_ready, 2)
            own.mark(dve.memset(k_rot[:, :, 0:NOPE], 0.0))
            latents((0, 1))
            rotate_key(0)
            split_to(N_KV)
            latents_gain(0)
            latents_low(0)
            latents((2,))
            split_to(N_UQ + 1)
            latents((3,))
            rotate_key(1)
            values_low(0)
            latents_gain(1)
            latents_low(1)
            dve.wait_ge(krot_turned, 2)
            queries(0)
            values_low(1)
            queries(1)

            def m_query(h):
                z = h % 2
                dve.wait_ge(m_qk_hi, 2 * h + 1)
                dve.scalar_tensor_tensor(mq_lo[0:HE, z, :], ps[0:HE, 0, :], MLA_SCALE, mq_hi[0:HE, z, :].bitcast(F32),
                                         ALU.mult, ALU.subtract).then_inc(m_qk_ready, 1)

            def m_key(h):
                z = h % 2
                dve.wait_ge(m_qk_hi, 2 * h + 2)
                dve.tensor_tensor(mk_lo[0:NOPE, z, :], ps[0:NOPE, 1, :], mk_hi[0:NOPE, z, :].bitcast(F32),
                                  ALU.subtract).then_inc(m_qk_ready, 1)

            m_query(0)
            m_key(0)
            for u in range(MU + 4):
                if u % KT == 2 and u // KT + 1 < HM:
                    m_key(u // KT + 1)
                if u < MU:
                    dve.wait_ge(m_scores, u + 1)
                    dve.tensor_reduce(mla_nm[:, u:u + 1], ps[:, 2 + u % 3, :], AXIS.X, ALU.max, negate=True)\
                        .then_inc(m_max, 1)
                v = u - 1
                if 0 <= v < MU:
                    dve.wait_ge(m_exp, v + 1)
                    own.mark(dve.reciprocal(mla_z[:, v:v + 1], mla_z[:, v:v + 1]))
                    own.settle()
                    dve.tensor_scalar(mp[:, v % 3, :], mp[:, v % 3, :], mla_z[:, v:v + 1], None, ALU.mult)\
                        .then_inc(m_normed, 1)
                v = u - 3
                if 0 <= v < MU:
                    dve.wait_ge(m_pt_hi, v + 1)
                    dst = (slice(None), v // 2 % 2, slice(None), slice(v % 2 * P, v % 2 * P + P))
                    dve.tensor_tensor(mpt_lo[dst], ps[:, 5 + v % 2, :].rearrange("p (c n) -> p c n", c=KT),
                                      mpt_hi[dst].bitcast(F32), ALU.subtract).then_inc(m_pt_ready, 1)
                if u % KT == 1 and u // KT + 1 < HM:
                    m_query(u // KT + 1)
                if u in (11, 15, 19, 23):
                    split_to(N_D0 + u // KT - 2)

            split_to(N_D0 + 10)
            for t in range(KT):
                dve.wait_ge(v0_hi_ready, t + 1)
                dve.tensor_tensor(v0_lo[:, t, :], ps[:, 2 * t + 1, 0:GW], v0_hi[:, t, :].bitcast(F32), ALU.subtract)\
                    .then_inc(v0_ready, 1)

            def rotate_dilated(view, t0, nt, heads, signal):
                sh = [P, nt, heads, MP]
                tmp = [rot_d[:, j, 0:nt * heads * MP].rearrange("p (t h e) -> p t h e", t=nt, h=heads)
                       for j in range(4)]
                c = cos_p[:, t0:t0 + nt, :].unsqueeze(2).broadcast_to(sh)
                s = sin_p[:, t0:t0 + nt, :].unsqueeze(2).broadcast_to(sh)
                rotate(view[:, :, :, 0:MP], view[:, :, :, MP:2 * MP], c, s, tmp, signal)

            dve.wait_ge(d0_copied, KT)
            for t in (0, 2):
                if t:
                    dve.wait_ge(d0_rotated, 1)
                rotate_dilated(qk0[:, t:t + 2, :].rearrange("p t (h e) -> p t h e", e=E), t, 2, 2 * HG, d0_rotated)
            split_to(N_V12 + 2)

            def d_operands(i):
                kind, g, _, bank, _ = PREP[i]
                parts = [(dq_lo[:, g, :], ps[:, bank, :], dq_hi[:, g, :], True)]
                parts += [(kz_lo[a * E:a * E + E, g, a, :], ps[a * E:a * E + E, bank + 1, :],
                           kz_hi[a * E:a * E + E, g, a, :], False) for a in range(2)]
                for dst, src, hi, scaled in parts:
                    dve.wait_ge(d_qk_hi, 3 * i + 1 if scaled else 3 * (i + 1))
                    if kind == "strided":
                        dst, hi = (y.rearrange("p (r l) -> p r l", r=DIL) for y in (dst, hi))
                        src = src.rearrange("p (l r) -> p r l", r=DIL)
                    if scaled:
                        dve.scalar_tensor_tensor(dst, src, DIL_SCALE, hi.bitcast(F32), ALU.mult, ALU.subtract)\
                            .then_inc(d_qk_ready, 1)
                    else:
                        dve.tensor_tensor(dst, src, hi.bitcast(F32), ALU.subtract).then_inc(d_qk_ready, 1)

            def d_max_unit(v):
                kind, p, a, t = D_UNITS[v]
                s = v % 3
                dve.wait_ge(d_scores, v + 1)
                if v >= 3:
                    dve.wait_ge(d_pt_done, v - 2)
                if kind == "local":
                    c = chunks(t)
                    w = len(c) * P
                    rel = c[0] - t + 1
                    own.mark(dve.tensor_tensor(dp[:, s, 0:w], ps[:, 2 + s, 0:w],
                                               mask0[:, rel:rel + len(c), :].rearrange("p c n -> p (c n)"), ALU.add))
                    own.settle()
                    dve.tensor_reduce(dil_nm[:, 0, p, t, a:a + 1], dp[:, s, 0:w], AXIS.X, ALU.max, negate=True)\
                        .then_inc(d_max, 1)
                else:
                    view = "p (g a n) -> p g a n"
                    own.mark(dve.tensor_tensor(dp[:, s, :].rearrange(view, g=2, a=2),
                                               ps[:, 2 + s, :].rearrange(view, g=2, a=2),
                                               mask12[:, :, :].unsqueeze(2).broadcast_to([P, 2, 2, P]), ALU.add))
                    own.settle()
                    dve.tensor_reduce(dil_nm[:, 1, p, t, :],
                                      dp[:, s, :].rearrange("p (g a n) -> p a g n", g=2, a=2), AXIS.XY,
                                      ALU.max, negate=True).then_inc(d_max, 1)

            def d_pt_low(v):
                dve.wait_ge(d_pt_hi, v + 1)
                dve.tensor_tensor(pt_view(dpt_lo, v), pt_bank(v), pt_view(dpt_hi, v).bitcast(F32), ALU.subtract)\
                    .then_inc(d_pt_ready, 1)

            def spread_stats(p):
                dve.wait_ge(d_exp, N_LOCAL + 2 * KT * (p + 1))
                dve.wait_ge(d_turned, len(PREP))
                for j, stat_ in enumerate((dil_nm, dil_z)):
                    for s in range(2):
                        dve.tensor_copy(mix_cols[:, p, 2 * j + s, :].rearrange("p (t a e) -> p t a e", t=KT, a=2, e=E),
                                        stat_[:, s, p, :, :].unsqueeze(3).broadcast_to([P, KT, 2, E]))\
                            .then_inc(mix_wide, 1)

            dve.wait_ge(kz_clear, 4)
            d_operands(0)
            qk12_heads = qk12[:, :, :, :].rearrange("p t m (h e) -> p t (m h) e", e=E)
            split_to(N_V12 + 3)
            for v in range(len(D_UNITS) + 5):
                if v in PREP_AT:
                    if v >= 3:
                        d_pt_low(v - 3)
                    for i in PREP_AT[v]:
                        d_operands(i)
                if v < len(D_UNITS):
                    d_max_unit(v)
                if 0 <= v - 3 < len(D_UNITS) and v not in PREP_AT:
                    d_pt_low(v - 3)
                if v in (24, 25):
                    spread_stats(v - 24)
                if v in ROTATE_AT:
                    t = ROTATE_AT.index(v)
                    if t == 0:
                        dve.wait_ge(d12_copied, KT)
                        dve.wait_ge(d0_rotated, 2)
                    else:
                        dve.wait_ge(d12_rotated, t)
                    rotate_dilated(qk12_heads[:, t:t + 1, :, :], t, 1, 4 * HG, d12_rotated)
                for r in V12_COPIES.get(v, ()):
                    dve.wait_ge(v12_hi_ready, r + 1)
                    hi, lo = v12(r)
                    dve.tensor_tensor(lo, ps[:, r % 2, :], hi.bitcast(F32), ALU.subtract).then_inc(v12_ready, 1)
                if 24 <= v < 28:
                    split_to(N_MRG + v - 24)

            def mix_scales(p):
                dve.wait_ge(mix_copied, 4 * (p + 1))
                if p:
                    dve.wait_ge(mix_diff, 2 * p)
                own.mark(dve.tensor_tensor(mix_max[:, :], mix[:, p, 0, :], mix[:, p, 2, :], ALU.min))
                own.settle()
                dve.tensor_tensor(mix[:, p, 0, :], mix_max[:, :], mix[:, p, 0, :], ALU.subtract).then_inc(mix_diff, 1)
                dve.tensor_tensor(mix[:, p, 2, :], mix_max[:, :], mix[:, p, 2, :], ALU.subtract).then_inc(mix_diff, 1)

            def mix_outputs(p):
                dve.wait_ge(mix_exp, 2 * (p + 1))
                dve.wait_ge(u_copied, 4 + 4 * KT)
                e0, z0, e12, z12 = (mix[:, p, j, :] for j in range(4))
                own.mark(dve.tensor_tensor(z0, z0, e0, ALU.mult))
                own.mark(dve.tensor_tensor(z12, z12, e12, ALU.mult))
                own.mark(dve.tensor_tensor(u0[:, p, :], u0[:, p, :], e0, ALU.mult))
                own.mark(dve.tensor_tensor(u12[:, p, :], u12[:, p, :], e12, ALU.mult))
                own.settle()
                own.mark(dve.tensor_tensor(z0, z0, z12, ALU.add))
                own.mark(dve.tensor_tensor(u12[:, p, :], u12[:, p, :], u0[:, p, :], ALU.add))
                own.settle()
                own.mark(dve.reciprocal(z12, z0))
                own.settle()
                dve.tensor_tensor(u12[:, p, :], u12[:, p, :], z12, ALU.mult).then_inc(mixed, 1)

            for hf in range(2):
                n = N_MRG + hf * MRG
                ga, gb, om, od = M_BANKS[hf]
                if hf == 0:
                    mix_scales(0)
                    mix_scales(1)
                    dve.wait_ge(om_hi_ready, 1)
                    dve.tensor_tensor(om_lo[:, :, :], o_mla[:, :, :], om_hi[:, :, :].bitcast(F32), ALU.subtract)\
                        .then_inc(om_ready, 1)
                split_to(n + 7)
                if hf == 0:
                    mix_outputs(0)
                    mix_outputs(1)
                split_to(n + 10)
                if hf == 0:
                    dve.wait_ge(od_hi_ready, 1)
                    dve.wait_ge(mixed, 2)
                    dve.tensor_tensor(od_lo[:, :, :], u12[:, :, :], od_hi[:, :, :].bitcast(F32), ALU.subtract)\
                        .then_inc(od_ready, 1)
                split_to(n + 13)
                dve.wait_ge(w_used, n + 10)
                dve.wait_ge(ga_ready, KT * (hf + 1))
                for t in range(KT):
                    dve.tensor_tensor(sg_a[:, t, :], sg_a[:, t, :], ps[:, om + t, :], ALU.mult).then_inc(om_gated, 1)
                if hf:
                    for c in range(LEAD):
                        split_a(1, 0, c, c)
                    down_chunk(1, 0, 0)
                dve.wait_ge(w_used, n + 11)
                dve.wait_ge(gb_ready, KT * (hf + 1))
                for t in range(KT):
                    dve.tensor_tensor(sg_b[:, t, :], sg_b[:, t, :], ps[:, od + t, :], ALU.mult).then_inc(od_gated, 1)
                dve.wait_ge(od_gated, KT * (hf + 1))
                dve.wait_ge(om_gated, KT * (hf + 1))
                for t in range(KT):
                    dve.tensor_tensor(sg_a[:, t, :], sg_a[:, t, :], sg_b[:, t, :], ALU.add).then_inc(merged, 1)
                split_to(n + 14)
            down_chunk(1, 0, 1)
            down(1)
            gate_up(1)
            down(2)

        @block.tensor
        def _(pe):
            def product(dst, a, b, start, stop, **kw):
                (a_h, a_l), (b_h, b_l) = a, b
                pe.matmul(dst, a_h, b_h, start=start, stop=False, **kw)
                pe.matmul(dst, a_h, b_l, start=False, stop=False, **kw)
                return pe.matmul(dst, a_l, b_h, start=False, stop=stop, **kw)

            def turn(dst, src):
                n = src.shape[0]
                return pe.transpose(dst, src, ident[0:n, 0:n])

            def w(n, a, b):
                return w_hi[:, n % RING, a:b], w_lo[:, n % RING, a:b]

            def h(k, tokens):
                return h_hi[:, k, tokens], h_lo[:, k, tokens]

            def arrived(n):
                pe.wait_ge(lo_ready, n + 1)

            def turn_x(m):
                s, t = m // 4, m % 4
                pe.wait_ge(xn_ready, m + 1)
                b = x_bank(s, t)
                for c in range(KD):
                    i = turn(ps[:, b + c // 4, c % 4 * P:(c % 4 + 1) * P], xn[:, c * P:(c + 1) * P])
                i.then_inc(x_turned, 1)

            def turn_ada(v, acc=ada_acc):
                pe.wait_ge(ada_added, v * KD + KD)
                for c in range(KD):
                    i = turn(ps[:, c // 4, c % 4 * P:(c % 4 + 1) * P], acc[:, c * P:(c + 1) * P])
                i.then_inc(ada_turned, 1)

            def spread_gain(s):
                pe.wait_ge(gates_ready, 3)
                for c in range(KD):
                    i = pe.matmul(ps[:, G_BANK[s] + c // 4, c % 4 * P:(c % 4 + 1) * P],
                                  gate_col[:, s, c:c + 1].broadcast_to([P, P]), ident[:, :], start=True, stop=True)
                i.then_inc(g_spread, 1)

            def gate_up(g):
                n0, f0 = GU_BASE[g], KF * g

                def block_product(s_n, bank, tokens):
                    for k in range(KD):
                        i = product(ps[:, bank, tokens], w(s_n, k * P, (k + 1) * P), h(k, tokens), k == 0, k == KD - 1)
                    return i

                for half in range(2):
                    if half and g == 0:
                        pe.wait_ge(residue_ready, 1)
                        pe.wait_ge(h_ready, 3)
                        pe.matmul(ps[:, 2, 0:P], residue[0:DIL, :], residue[0:DIL, :], start=True, stop=True)\
                            .then_inc(residue_mult, 1)
                    if half and g:
                        turn_x(11)
                    pe.wait_ge(h_ready, 8 * g + 2 * half + 2)
                    tokens = slice(half * 256, half * 256 + 256)
                    for b in range(4):
                        if half == 0:
                            if g and b == 3:
                                turn_x(10)
                            arrived(n0 + b)
                        i = block_product(n0 + b, 4 + b, tokens)
                        if half:
                            i.then_inc(w_used, 1)

                def tile(i, q, ada):
                    pe.wait_ge(a_ready, i * 2 + (f0 + q - 1))
                    for b in range(2):
                        s_n = n0 + 2 * q + b
                        arrived(i * 4 + s_n)
                        block_product(s_n, 4 + 2 * q + b, slice(0, T)).then_inc(w_used, 1)

                with pe.Fori(1, 8) as i:
                    for q in range(2):
                        tile(i, q, False)
                    if g == 0:
                        pe.wait_ge(ada_summed, i + 1)
                        turn_ada(i + 1)
                with pe.Fori(8, KF // 2 - 1) as i:
                    for q in range(2):
                        tile(i, q, False)
                spread_gain(2 * g)
                for q in range(2):
                    tile(KF // 2 - 1, q, False)

            def down(d):
                nch, n0 = DN_CHUNKS[d], DN_BASE[d]

                def chunk(hf, c, s_c):
                    s_n = n0 + hf * nch + s_c
                    arrived(c + (n0 + hf * nch))
                    pe.wait_ge(a_lo_ready, c + (DN_COUNT[d] + hf * nch + 1))
                    slot = (hf * nch + s_c) % RING
                    for t in range(2):
                        a = tuple(y[:, slot, t * P:(t + 1) * P] for y in (a_hi, a_lo))
                        for b in range(2):
                            i = product(ps[:, y_bank(d, 2 * hf + t) + b, :], a, w(s_n, b * 512, (b + 1) * 512),
                                        s_c == 0, s_c == nch - 1)
                    i.then_inc(w_used, 1)

                def last_chunks(c0):
                    for t in range(2):
                        for c in (c0, c0 + 1):
                            arrived(n0 + nch + c)
                            pe.wait_ge(a_lo_ready, DN_COUNT[d] + nch + c + 1)
                            slot = (nch + c) % RING
                            a = tuple(y[:, slot, t * P:(t + 1) * P] for y in (a_hi, a_lo))
                            for b in range(2):
                                i = product(ps[:, y_bank(d, 2 + t) + b, :], a,
                                            w(n0 + nch + c, b * 512, (b + 1) * 512), False, c == nch - 1)
                            if t:
                                i.then_inc(w_used, 1)
                        if t == 0:
                            i.then_inc(third_summed, 1)

                def chunk_loop(hf, first, last):
                    with pe.Fori(0, (last - first) // 4) as i:
                        for j in range(first, first + 4):
                            chunk(hf, i * 4 + j, j)

                if d != 1:
                    pe.wait_ge(g_ready, d + 1)
                if nch > 8:
                    for c in range(4):
                        chunk(0, c, c)
                    chunk_loop(0, 4, 20)
                    for c in range(20, nch):
                        chunk(0, c, c)
                else:
                    pe.wait_ge(om_gated, 2 * KT)
                    for c in range(3):
                        chunk(0, c, c)
                    turn_merged(1)
                    chunk(0, 3, 3)
                    chunk(0, 4, 4)
                    pe.wait_ge(m_t_ready, KD)
                    spread_gain(1)
                    for c in range(5, nch):
                        chunk(0, c, c)
                for c in range(min(8, nch - 2)):
                    if c == 0 and d == 1:
                        pe.wait_ge(g_ready, 2)
                    if c == 0 and d != 1:
                        pe.wait_ge(a_ready, KF * (1 + d // 2))
                    chunk(1, c, c)
                    if d < 2 and c in (4, 5):
                        turn_x(4 * (d + 1) + c - 4)
                if nch > 8:
                    chunk_loop(1, 8, 20)
                last_chunks(nch - 2)

            pe.wait_ge(consts_ready, 1)
            pe.wait_ge(rows_a_in, 16 * 5)
            turn(ps[:, 0, 0:RA_N], rows_a[0:RA_N, :]).then_inc(rows_turned, 1)
            turn_x(0)
            turn_x(1)
            pe.wait_ge(rows_b_in, 16 * 5)
            turn(ps[:, 1, 0:RB_N], rows_b[0:RB_N, :]).then_inc(rows_turned, 1)
            turn_x(2)
            pe.wait_ge(cols_ready, 2)
            turn_ada(0)
            pe.wait_ge(ada_summed, 1)
            turn_ada(1, upd)
            pe.wait_ge(ada_summed, 2)
            turn_x(3)
            gate_up(0)
            down(0)

            def latents(tiles, blocks):
                for b in blocks:
                    n = N_LAT + b
                    if 0 in tiles:
                        arrived(n)
                    for kk in range(2):
                        k = 2 * b + kk
                        for t in tiles:
                            i = product(ps[:, t, 0:LAT], h(k, slice(t * P, (t + 1) * P)),
                                        w(n, kk * LAT, (kk + 1) * LAT), k == 0, k == KD - 1)
                    if KT - 1 in tiles:
                        i.then_inc(w_used, 1)
                    elif b == KD // 2 - 1:
                        i.then_inc(lat_summed, 1)

            def turn_latents(half):
                pe.wait_ge(krot_turned, half + 1)
                for t in (2 * half, 2 * half + 1):
                    pe.wait_ge(lat_normed, t + 1)
                    for c in range(3):
                        turn(ps[:, t, c * P:(c + 1) * P], lat[:, t, c * P:(c + 1) * P])
                    turn(ps[0:HE, t, 3 * P:4 * P], k_rot[:, t, :]).then_inc(lat_turned, 1)

            ukv = [y[:, :].rearrange("p (h e) -> p h e", e=P) for y in (ukv_hi, ukv_lo)]

            def values(half):
                arrived(N_KV)
                pe.wait_ge(c_ready, half + 1)
                for t in (2 * half, 2 * half + 1):
                    if half:
                        pe.wait_ge(mv_ready, t - 1)
                    i = product(ps[:, 4 + t % 2, :].rearrange("p (h e) -> p h e", e=VD),
                                tuple(y[:, 2, t * P:(t + 1) * P] for y in (c_hi, c_lo)),
                                tuple(y[:, :, NOPE:P] for y in ukv), True, True)
                    i.then_inc(mv_done if t < KT - 1 else w_used, 1)

            def queries(half):
                arrived(N_UQ + 1)
                for t in (2 * half, 2 * half + 1):
                    if half:
                        pe.wait_ge(q_copied, t - 1)
                    for k in range(2):
                        for b in range(2):
                            i = product(ps[:, UQ_BANK[t] + b, 0:384],
                                        tuple(y[:, k, t * P:(t + 1) * P] for y in (c_hi, c_lo)),
                                        w(N_UQ + k, b * 384, (b + 1) * 384), k == 0, k == 1)
                        if t == KT - 1:
                            i.then_inc(w_used, 1)
                    if t < KT - 1:
                        i.then_inc(uq_done, 1)

            pe.wait_ge(h_ready, 6)
            latents((0, 1), range(3))
            turn_x(6)
            latents((0, 1), range(3, KD // 2))
            turn_x(7)
            pe.wait_ge(h_ready, 7)
            latents((2,), range(KD // 2))
            turn_latents(0)
            pe.wait_ge(h_ready, 8)
            latents((3,), range(KD // 2))
            values(0)
            queries(0)
            turn_latents(1)
            values(1)
            queries(1)

            def m_operands(hd):
                if hd:
                    pe.wait_ge(m_qk_ready, 2 * hd)
                else:
                    pe.wait_ge(q_copied, KT - 1)
                product(ps[:, 1, :], tuple(y[:, hd * P:(hd + 1) * P] for y in (ukv_hi, ukv_lo)),
                        tuple(y[:, 2, :] for y in (c_hi, c_lo)), True, True)
                if hd == 0:
                    pe.wait_ge(q_rotated, 2)
                for t in range(KT):
                    i = turn(ps[0:HE, 0, t * P:(t + 1) * P], q_nat[:, t, hd * HE:(hd + 1) * HE])
                i.then_inc(m_turned, 1)

            def m_values(j):
                hd, half = j // 2, j % 2
                pe.wait_ge(m_pt_ready, 2 * j + 2)
                if half == 0 and hd:
                    pe.wait_ge(m_out_copied, hd)
                for c in range(KT):
                    i = product(ps[:, 7, half * 256:half * 256 + 256],
                                tuple(y[:, c, hd // 2 * P:(hd // 2 + 1) * P] for y in (mv_hi, mv_lo)),
                                tuple(y[:, j % 2, c, :] for y in (mpt_hi, mpt_lo)), c == 0, c == KT - 1)
                i.then_inc(m_pv, 1)

            m_operands(0)
            for u in range(MU + 5):
                if u % KT == 1 and u // KT + 1 < HM:
                    m_operands(u // KT + 1)
                if u < MU:
                    hd, t = u // KT, u % KT
                    pe.wait_ge(m_qk_ready, 2 * hd + 2)
                    if u >= 3:
                        pe.wait_ge(m_exp, u - 2)
                    product(ps[:, 2 + u % 3, :], tuple(y[0:HE, hd % 2, t * P:(t + 1) * P] for y in (mq_hi, mq_lo)),
                            tuple(y[0:HE, hd % 2, :] for y in (mk_hi, mk_lo)), True, True).then_inc(m_scores, 1)
                v = u - 3
                if 0 <= v < MU:
                    pe.wait_ge(m_normed, v + 1)
                    if v >= 2:
                        pe.wait_ge(m_pt_ready, v - 1)
                    for c in range(KT):
                        i = turn(ps[:, 5 + v % 2, c * P:(c + 1) * P], mp[:, v % 3, c * P:(c + 1) * P])
                    i.then_inc(m_pt_done, 1)
                v = u - 5
                if v >= 0 and v % 2:
                    m_values(v // 2)

            for k in range(KD):
                n = N_D0 + k
                arrived(n)
                if k == 0:
                    pe.wait_ge(m_out_copied, HM)
                for t in range(KT):
                    for b, (lo, hi) in enumerate(((0, 2 * GW), (2 * GW, 3 * GW))):
                        i = product(ps[:, 2 * t + b, 0:hi - lo], h(k, slice(t * P, (t + 1) * P)), w(n, lo, hi),
                                    k == 0, k == KD - 1)
                i.then_inc(w_used, 1)
            for k in range(KD):
                n = N_D12 + k
                arrived(n)
                for t in range(KT):
                    if k == 0:
                        pe.wait_ge(d0_copied, t + 1)
                        pe.wait_ge(v0_ready, t + 1)
                    for b in range(2):
                        i = product(ps[:, 2 * t + b, :], h(k, slice(t * P, (t + 1) * P)), w(n, b * 512, (b + 1) * 512),
                                    k == 0, k == KD - 1)
                i.then_inc(w_used, 1)

            def d_operands(i):
                kind, g, p, bank, _ = PREP[i]
                if kind == "local":
                    pe.wait_ge(d0_rotated, 2)
                else:
                    pe.wait_ge(d12_rotated, KT)
                pe.wait_ge(*((d12_copied, 1), (d12_copied, KT), (v12_ready, 2), (d_max, 15), (v12_ready, 4),
                             (d_max, 20))[i])
                for m in range(2):
                    for t in range(KT):
                        if kind == "local":
                            src = qk0[:, t, m * GW + p * P:m * GW + (p + 1) * P]
                        else:
                            src = qk12[:, t, m, g * GW + p * P:g * GW + (p + 1) * P]
                        j = turn(ps[:, bank + m, t * P:(t + 1) * P], src)
                j.then_inc(d_turned, 1)

            def d_scores_unit(v):
                kind, p, a, t = D_UNITS[v]
                if v >= 3:
                    pe.wait_ge(d_max, v - 2)
                else:
                    pe.wait_ge(d12_copied, 3)
                bank = 2 + v % 3
                if kind == "local":
                    pe.wait_ge(d_qk_ready, 3 * (p + 1))
                    c = chunks(t)
                    cols = slice(c[0] * P, (c[-1] + 1) * P)
                    product(ps[:, bank, 0:len(c) * P], tuple(y[:, p, t * P:(t + 1) * P] for y in (dq_hi, dq_lo)),
                            tuple(y[:, p, a, cols] for y in (kz_hi, kz_lo)), True, True).then_inc(d_scores, 1)
                    return
                if p == 0:
                    pe.wait_ge(d_qk_ready, 3 * 4)
                for g in range(2):
                    if p:
                        pe.wait_ge(d_qk_ready, 3 * (5 + g))
                    i = product(ps[:, bank, g * 256:(g + 1) * 256].rearrange("p (a n) -> p a n", a=2),
                                tuple(y[:, g, t * P:(t + 1) * P] for y in (dq_hi, dq_lo)),
                                tuple(y[:, g, :, t * P:(t + 1) * P] for y in (kz_hi, kz_lo)), True, True)
                i.then_inc(d_scores, 1)

            def d_turn_unit(v):
                kind, _, _, t = D_UNITS[v]
                n = len(chunks(t)) if kind == "local" else 4
                pe.wait_ge(d_exp, v + 1 if v < N_LOCAL else N_LOCAL + 2 * (v - N_LOCAL + 1))
                if v >= 2:
                    pe.wait_ge(d_pt_ready, v - 1)
                else:
                    pe.wait_ge(d_qk_ready, 6)
                for c in range(n):
                    i = turn(ps[:, 5 + v % 2, c * P:(c + 1) * P], dp[:, v % 3, c * P:(c + 1) * P])
                i.then_inc(d_pt_done, 1)

            def d_values(v):
                kind, p, a, t = D_UNITS[v]
                pe.wait_ge(d_pt_ready, v + 1)
                if kind == "local":
                    for kc in pv0_steps(t):
                        q = chunks(kc)
                        cols = slice(q[0] * P, (q[-1] + 1) * P)
                        if kc == 0 and v >= KT:
                            pe.wait_ge(u_copied, v // KT)
                        product(ps[:, 7, cols], tuple(y[:, kc, p * P:(p + 1) * P] for y in (v0_hi, v0_lo)),
                                tuple(y[:, kc, cols] for y in (dpt_hi, dpt_lo)), kc == 0, kc == KT - 1,
                                skip_group_check=True).then_inc(pv0_used, 1)
                    return
                wv = v - N_LOCAL
                pe.wait_ge(v12_ready, t + 1)
                pe.wait_ge(u_copied, 4 + 2 * wv)
                for g in range(2):
                    i = product(ps[:, 7, t % 2 * 256:(t % 2 + 1) * 256],
                                tuple(y[:, g * GW + p * P:g * GW + (p + 1) * P] for y in v12(t)),
                                tuple(y[:, wv % KT, g * 256:(g + 1) * 256] for y in (dpt_hi, dpt_lo)),
                                g == 0, g == 1)
                i.then_inc(pv12_used, 1)

            def v12_product(m):
                k, r = m % 16 // 2, m // 16 * 2 + m % 2
                n = N_V12 + k // 2
                if m < 16:
                    arrived(n)
                if m == 0:
                    pe.wait_ge(d_qk_ready, 3)
                if m == 16:
                    pe.wait_ge(d_qk_ready, 9)
                i = product(ps[:, r % 2, :], h(k, slice(r, T, DIL)), w(n, k % 2 * 512, (k % 2 + 1) * 512),
                            k == 0, k == KD - 1)
                if m == 15:
                    i.then_inc(v12_half, 1)
                if m >= 16 and m % 4 == 3:
                    i.then_inc(w_used, 1)

            def turns_and_values(v):
                if 0 <= v - 3 < len(D_UNITS):
                    d_turn_unit(v - 3)
                if v - 5 >= 0:
                    d_values(v - 5)

            def spread_stats(p):
                pe.wait_ge(mix_wide, 4 * (p + 1))
                for j, src in enumerate((0, 2, 1, 3)):
                    for t in range(KT):
                        i = pe.matmul(ps[:, 4 * p + j, t * P:(t + 1) * P], mix_cols[:, p, src, t * P:(t + 1) * P],
                                      ident[:, :], start=True, stop=True)
                i.then_inc(mix_spread, 1)

            d_operands(0)
            m = 0
            for v in range(len(D_UNITS) + 5):
                if v in PREP_AT:
                    turns_and_values(v)
                    for i in PREP_AT[v]:
                        d_operands(i)
                for m in range(m, m + V12_COUNTS.get(v, 0)):
                    v12_product(m)
                    m += 1
                if v < len(D_UNITS):
                    d_scores_unit(v)
                if v not in PREP_AT:
                    turns_and_values(v)
                if v == 26:
                    pe.wait_ge(d_max, len(D_UNITS))
                    spread_stats(0)

            pe.wait_ge(u_copied, 4 + 4 * KT)
            spread_stats(1)

            def turn_merged(hf):
                pe.wait_ge(merged, KT * (hf + 1))
                for c in range(4):
                    for t in range(KT):
                        i = turn(ps[:, c, t * P:(t + 1) * P], sg_a[:, t, c * P:(c + 1) * P])
                    i.then_inc(m_t_done, 1)

            for hf in range(2):
                n = N_MRG + hf * MRG
                ga, gb, om, od = M_BANKS[hf]
                for m, bank in ((0, ga), (1, gb)):
                    if hf == 0:
                        pe.wait_ge(mix_copied, 4 * (m + 1))
                    elif m == 1:
                        pe.wait_ge(m_t_ready, 4)
                    for b in range(KD // 2):
                        if hf and m == 0 and b == 2:
                            turn_merged(0)
                        arrived(n + 4 * m + b)
                        for kk in range(2):
                            k = 2 * b + kk
                            for t in range(KT):
                                if hf and m == 0 and k == 0:
                                    pe.wait_ge(od_gated, t + 1)
                                i = product(ps[:, bank + t, :], h(k, slice(t * P, (t + 1) * P)),
                                            w(n + 4 * m + b, kk * 512, (kk + 1) * 512), k == 0, k == KD - 1)
                        i.then_inc(w_used, 1)
                pe.wait_ge(ga_ready, KT * (hf + 1))
                pe.wait_ge(om_ready, 1)
                for b in range(2):
                    arrived(n + 8 + b)
                    for kk in range(2):
                        c = 2 * b + kk
                        for t in range(KT):
                            i = product(ps[:, om + t, :], tuple(y[:, c, t * P:(t + 1) * P] for y in (om_hi, om_lo)),
                                        w(n + 8 + b, kk * 512, (kk + 1) * 512), c == 0, c == 3)
                    i.then_inc(w_used, 1)
                pe.wait_ge(gb_ready, KT * (hf + 1))
                pe.wait_ge(od_ready, 1)
                arrived(n + 10)
                for c in range(2):
                    for t in range(KT):
                        i = product(ps[:, od + t, :], tuple(y[:, c, t * P:(t + 1) * P] for y in (od_hi, od_lo)),
                                    w(n + 10, c * 512, (c + 1) * 512), c == 0, c == 1)
                i.then_inc(w_used, 1)
            down(1)
            gate_up(1)
            down(2)


def kernel(**inputs):
    import concourse.bacc as bacc
    from concourse.bass_utils import run_bass_kernel_spmd

    nc = bacc.Bacc("TRN2", target_bir_lowering=False, num_devices=1)
    arrays, args = {}, {}
    for name in inputs:
        a = np.ascontiguousarray(inputs[name])
        arrays[f"in_{name}"] = a
        args[name] = nc.dram_tensor(f"in_{name}", a.shape, mybir.dt.from_np(a.dtype), kind="ExternalInput").ap()
    shape = inputs["x"].shape
    out = nc.dram_tensor("out", shape, F32, kind="ExternalOutput").ap()
    encoder_block(nc, args, out)
    r = run_bass_kernel_spmd(nc, [arrays], core_ids=[0])
    return r.results[0]["out"]
```
